# Optimizing a Trainium2 kernel written in Bass

```python
import math
import jax
import jax.numpy as jnp
from jax import lax

D_MODEL = 1024
BATCH = 1
SEQ = 256
DEPTH = 4
DEC_BATCH = 8
DEC_SEQ = 4
PAST_LEN = 1024
PAGE_SIZE = 128

N_MIXERS = 3
N_SSD = (DEPTH + 2) // 3
N_SWA = (DEPTH + 1) // 3
N_DIFF = DEPTH // 3

D_FF = -((-8 * D_MODEL) // (3 * 256)) * 256

SSM_EXPAND = 2
D_INNER = SSM_EXPAND * D_MODEL
SSM_HEAD_DIM = 64
SSM_HEADS = D_INNER // SSM_HEAD_DIM
SSM_GROUPS = 4
D_STATE = 128
CONV_W = 4
CONV_DIM = D_INNER + 2 * SSM_GROUPS * D_STATE
SSM_IN_DIM = 2 * D_INNER + 2 * SSM_GROUPS * D_STATE + SSM_HEADS
SSD_CHUNK = 128

HEAD_DIM = 64
N_ATTN_HEADS = 12
NUM_BUCKETS = 32
MAX_DISTANCE = 2048

SWA_GROUPS = ((128, 1), (512, 4), (2048, 16))
SWA_HEADS_PER_GROUP = N_ATTN_HEADS // len(SWA_GROUPS)

DIFF_KV_HEADS = 4
DIFF_REP = N_ATTN_HEADS // DIFF_KV_HEADS
DIFF_V_DIM = 2 * HEAD_DIM
DIFF_QKV_DIM = N_ATTN_HEADS * 2 * HEAD_DIM + DIFF_KV_HEADS * 2 * HEAD_DIM + DIFF_KV_HEADS * DIFF_V_DIM
Q_BLOCK = 128

EPS = 1e-6

kernel_name = 'hybrid_ssd_dilated_diff_decoder_step'

def rmsnorm(x, g):
    xf = x.astype(jnp.float32)
    y = xf * lax.rsqrt(jnp.mean(xf * xf, axis=-1, keepdims=True) + EPS)
    return (y * g.astype(jnp.float32)).astype(x.dtype)

def rel_bucket(dist):
    max_exact = NUM_BUCKETS // 2
    d = jnp.maximum(dist, 0)
    df = jnp.maximum(d, 1).astype(jnp.float32)
    large = max_exact + (jnp.log(df / max_exact) / math.log(MAX_DISTANCE / max_exact)
                         * (NUM_BUCKETS - max_exact)).astype(jnp.int32)
    return jnp.where(d < max_exact, d, jnp.minimum(large, NUM_BUCKETS - 1))

def swiglu(h, w_in, w_out):
    g, u = jnp.split(h @ w_in, 2, axis=-1)
    return (jax.nn.silu(g) * u) @ w_out

def segsum(a):
    t = a.shape[-1]
    cs = jnp.cumsum(a, axis=-1)
    diff = cs[..., :, None] - cs[..., None, :]
    return jnp.where(jnp.tril(jnp.ones((t, t), bool)), diff, -jnp.inf)

def ssd_scan(x, dt, a, b, c, h0):
    bt, L, H, P = x.shape
    G, N = b.shape[-2:]
    R = H // G
    q = SSD_CHUNK if L % SSD_CHUNK == 0 else L
    nc = L // q
    xdt = (x * dt[..., None]).reshape(bt, nc, q, G, R, P)
    adt = jnp.transpose((dt * a).reshape(bt, nc, q, G, R), (0, 1, 3, 4, 2))
    b = b.reshape(bt, nc, q, G, N)
    c = c.reshape(bt, nc, q, G, N)
    a_cum = jnp.cumsum(adt, axis=-1)
    cb = jnp.einsum('bcign,bcjgn->bcgij', c, b)
    w = cb[:, :, :, None] * jnp.exp(segsum(adt))
    y_diag = jnp.einsum('bcgrij,bcjgrp->bcigrp', w, xdt)
    decay_states = jnp.exp(a_cum[..., -1:] - a_cum)
    states = jnp.einsum('bcjgn,bcgrj,bcjgrp->bcgrpn', b, decay_states, xdt)
    states = jnp.concatenate([h0.reshape(bt, 1, G, R, P, N), states], axis=1)
    chunk_a = jnp.pad(jnp.transpose(a_cum[..., -1], (0, 2, 3, 1)), ((0, 0), (0, 0), (0, 0), (1, 0)))
    new_states = jnp.einsum('bgrzc,bcgrpn->bzgrpn', jnp.exp(segsum(chunk_a)), states)
    y_off = jnp.einsum('bcign,bcgrpn,bcgri->bcigrp', c, new_states[:, :-1], jnp.exp(a_cum))
    y = (y_diag + y_off).reshape(bt, L, H, P)
    return y, new_states[:, -1].reshape(bt, H, P, N)

def ssd_mixer(h, conv_state, ssm_state, w_in, conv_w, conv_b, dt_bias, a_log, d_skip, norm_g, w_out):
    f32 = jnp.float32
    bt, L, _ = h.shape
    z, xbc, dt = jnp.split(h @ w_in, [D_INNER, D_INNER + CONV_DIM], axis=-1)
    ext = jnp.concatenate([conv_state.astype(xbc.dtype), xbc], axis=1)
    conv = conv_b + sum(ext[:, k:k + L] * conv_w[k] for k in range(CONV_W))
    new_conv = ext[:, L:]
    xs, bs, cs = jnp.split(jax.nn.silu(conv), [D_INNER, D_INNER + SSM_GROUPS * D_STATE], axis=-1)
    xh = xs.reshape(bt, L, SSM_HEADS, SSM_HEAD_DIM).astype(f32)
    dtf = jax.nn.softplus(dt.astype(f32) + dt_bias.astype(f32))
    a = -jnp.exp(a_log.astype(f32))
    y, new_state = ssd_scan(xh, dtf, a,
                            bs.reshape(bt, L, SSM_GROUPS, D_STATE).astype(f32),
                            cs.reshape(bt, L, SSM_GROUPS, D_STATE).astype(f32),
                            ssm_state.astype(f32))
    y = y + xh * d_skip.astype(f32)[:, None]
    gated = (y.reshape(bt, L, D_INNER) * jax.nn.silu(z.astype(f32))).reshape(bt, L, SSM_GROUPS, D_INNER // SSM_GROUPS)
    y = rmsnorm(gated, norm_g.reshape(SSM_GROUPS, D_INNER // SSM_GROUPS)).reshape(bt, L, D_INNER)
    return y.astype(h.dtype) @ w_out, new_conv, new_state.astype(ssm_state.dtype)

def swa_project(h, w_qkv, q_norm, k_norm):
    bt, L, _ = h.shape
    q, k, v = jnp.split(h @ w_qkv, 3, axis=-1)
    shape = (bt, L, N_ATTN_HEADS, HEAD_DIM)
    return rmsnorm(q.reshape(shape), q_norm), rmsnorm(k.reshape(shape), k_norm), v.reshape(shape)

def _to_classes(t, dil, blk, lp):
    bt, L = t.shape[:2]
    rest = t.shape[2:]
    t = jnp.pad(t, [(0, 0), (0, lp - L)] + [(0, 0)] * len(rest))
    t = jnp.moveaxis(t.reshape((bt, lp // dil, dil) + rest), 2, 1)
    return t.reshape((bt, dil, lp // (dil * blk), blk) + rest)

def _from_classes(t, L):
    bt, dil, nb, blk = t.shape[:4]
    rest = t.shape[4:]
    t = jnp.moveaxis(t.reshape((bt, dil, nb * blk) + rest), 1, 2)
    return t.reshape((bt, nb * blk * dil) + rest)[:, :L]

def _with_prev(t):
    prev = jnp.concatenate([jnp.zeros_like(t[:, :, :1]), t[:, :, :-1]], axis=2)
    return jnp.concatenate([prev, t], axis=3)

def dilated_group_prompt(q, k, v, bias_tab, win, dil):
    f32 = jnp.float32
    L = q.shape[1]
    steps = win // dil
    blk = steps
    span = dil * blk
    lp = -(-L // span) * span
    nb = lp // span
    qb = _to_classes(q, dil, blk, lp)
    kk = _with_prev(_to_classes(k, dil, blk, lp))
    vv = _with_prev(_to_classes(v, dil, blk, lp))
    s = jnp.einsum('bcnihd,bcnjhd->bcnhij', qb, kk).astype(f32) * (HEAD_DIM ** -0.5)
    i = jnp.arange(blk)[:, None]
    j = jnp.arange(2 * blk)[None, :]
    step = blk + i - j
    bias = bias_tab[rel_bucket(jnp.clip(step, 0, steps) * dil)].astype(f32)
    s = s + jnp.transpose(bias, (2, 0, 1))
    key_sub = jnp.arange(nb)[:, None, None] * blk + j[None] - blk
    valid = (step >= 0)[None] & (step <= steps)[None] & (key_sub >= 0)
    s = jnp.where(valid[None, None, :, None], s, -jnp.inf)
    lse = jax.nn.logsumexp(s, axis=-1)
    p = jnp.exp(s - lse[..., None])
    o = jnp.einsum('bcnhij,bcnjhd->bcnihd', p, vv.astype(f32))
    return _from_classes(o, L), _from_classes(jnp.swapaxes(lse, -1, -2), L)

def dilated_group_sample(q, k, v, buf, bias_tab, win, dil):
    f32 = jnp.float32
    T = q.shape[1]
    lb = buf.shape[1]
    k_ext = jnp.concatenate([buf[:, :, 0], k.astype(buf.dtype)], axis=1)
    v_ext = jnp.concatenate([buf[:, :, 1], v.astype(buf.dtype)], axis=1)
    steps = win // dil
    n = jnp.arange(steps + 1)
    idx = lb + jnp.arange(T)[:, None] - n[None, :] * dil
    valid = idx >= 0
    idx = jnp.maximum(idx, 0)
    kg = k_ext[:, idx]
    vg = v_ext[:, idx]
    s = jnp.einsum('bthd,btnhd->bthn', q, kg).astype(f32) * (HEAD_DIM ** -0.5)
    s = s + bias_tab[rel_bucket(n * dil)].astype(f32).T
    s = jnp.where(valid[:, None, :], s, -jnp.inf)
    lse = jax.nn.logsumexp(s, axis=-1)
    p = jnp.exp(s - lse[..., None])
    o = jnp.einsum('bthn,btnhd->bthd', p, vg.astype(f32))
    keep = min(win, lb + T)
    new_buf = jnp.concatenate([buf, jnp.stack([k, v], axis=2).astype(buf.dtype)], axis=1)[:, lb + T - keep:]
    return o, lse, new_buf

def swa_combine(outs, lses, w_out):
    alpha = jax.nn.softmax(jnp.stack(lses, axis=0), axis=0)
    o = jnp.concatenate([alpha[g][..., None] * outs[g] for g in range(len(outs))], axis=2)
    bt, L = o.shape[:2]
    return o.reshape(bt, L, -1).astype(w_out.dtype) @ w_out

def swa_prompt(h, w_qkv, q_norm, k_norm, w_out, rel_bias):
    q, k, v = swa_project(h, w_qkv, q_norm, k_norm)
    L = h.shape[1]
    outs, lses, bufs = [], [], []
    for g, (win, dil) in enumerate(SWA_GROUPS):
        sl = slice(g * SWA_HEADS_PER_GROUP, (g + 1) * SWA_HEADS_PER_GROUP)
        o, lse = dilated_group_prompt(q[:, :, sl], k[:, :, sl], v[:, :, sl], rel_bias[:, sl], win, dil)
        outs.append(o)
        lses.append(lse)
        keep = min(win, L)
        bufs.append(jnp.stack([k[:, L - keep:, sl], v[:, L - keep:, sl]], axis=2))
    return swa_combine(outs, lses, w_out), bufs

def swa_sample(h, bufs, w_qkv, q_norm, k_norm, w_out, rel_bias):
    q, k, v = swa_project(h, w_qkv, q_norm, k_norm)
    outs, lses, new_bufs = [], [], []
    for g, (win, dil) in enumerate(SWA_GROUPS):
        sl = slice(g * SWA_HEADS_PER_GROUP, (g + 1) * SWA_HEADS_PER_GROUP)
        o, lse, nbuf = dilated_group_sample(q[:, :, sl], k[:, :, sl], v[:, :, sl], bufs[g], rel_bias[:, sl], win, dil)
        outs.append(o)
        lses.append(lse)
        new_bufs.append(nbuf)
    return swa_combine(outs, lses, w_out), new_bufs

def diff_project(h, w_qkv, q_norm, k_norm):
    bt, L, _ = h.shape
    q, k, v = jnp.split(h @ w_qkv, [N_ATTN_HEADS * 2 * HEAD_DIM, (N_ATTN_HEADS + DIFF_KV_HEADS) * 2 * HEAD_DIM], axis=-1)
    q = rmsnorm(q.reshape(bt, L, DIFF_KV_HEADS, DIFF_REP, 2, HEAD_DIM), q_norm)
    k = rmsnorm(k.reshape(bt, L, DIFF_KV_HEADS, 2, HEAD_DIM), k_norm)
    return q, k, v.reshape(bt, L, DIFF_KV_HEADS, DIFF_V_DIM)

def diff_lambda_value(lam_p, lam_init):
    lp = lam_p.astype(jnp.float32)
    return jnp.exp(jnp.sum(lp[0] * lp[1])) - jnp.exp(jnp.sum(lp[2] * lp[3])) + lam_init

def diff_attend(q, k, v, q_pos, k_pos, lam, rel_bias):
    f32 = jnp.float32
    tq, tk = q.shape[1], k.shape[1]
    s = jnp.einsum('bigrmd,bjgmd->bgrmij', q, k).astype(f32) * (HEAD_DIM ** -0.5)
    dist = q_pos[:, None] - k_pos[None, :]
    bias = rel_bias[rel_bucket(dist)].astype(f32).reshape(tq, tk, DIFF_KV_HEADS, DIFF_REP)
    s = s + jnp.transpose(bias, (2, 3, 0, 1))[:, :, None]
    s = jnp.where(dist >= 0, s, -jnp.inf)
    p = jax.nn.softmax(s, axis=-1)
    a = p[:, :, :, 0] - lam * p[:, :, :, 1]
    return jnp.einsum('bgrij,bjgd->bigrd', a, v.astype(f32))

def diff_output(o, out_norm, lam_init, w_out):
    bt, L = o.shape[:2]
    o = rmsnorm(o.reshape(bt, L, N_ATTN_HEADS, DIFF_V_DIM), out_norm) * (1.0 - lam_init)
    return o.reshape(bt, L, -1).astype(w_out.dtype) @ w_out

def diff_prompt(h, w_qkv, q_norm, k_norm, lam_p, out_norm, w_out, rel_bias, lam_init):
    bt, L, _ = h.shape
    q, k, v = diff_project(h, w_qkv, q_norm, k_norm)
    lam = diff_lambda_value(lam_p, lam_init)
    nb = L // Q_BLOCK
    pos = jnp.arange(L)
    q_blocks = jnp.moveaxis(q.reshape((bt, nb, Q_BLOCK) + q.shape[2:]), 1, 0)
    o = lax.map(lambda a: diff_attend(a[0], k, v, a[1], pos, lam, rel_bias), (q_blocks, pos.reshape(nb, Q_BLOCK)))
    o = jnp.moveaxis(o, 0, 1).reshape(bt, L, DIFF_KV_HEADS, DIFF_REP, DIFF_V_DIM)
    return diff_output(o, out_norm, lam_init, w_out), k, v

def diff_sample(h, cache_k, cache_v, page_table, w_qkv, q_norm, k_norm, lam_p, out_norm, w_out, rel_bias, lam_init):
    bt, T, _ = h.shape
    q, k, v = diff_project(h, w_qkv, q_norm, k_norm)
    lam = diff_lambda_value(lam_p, lam_init)
    past_k = cache_k[page_table]
    past_k = past_k.reshape((bt, -1) + past_k.shape[3:])
    past_v = cache_v[page_table]
    past_v = past_v.reshape((bt, -1) + past_v.shape[3:])
    past = past_k.shape[1]
    k_all = jnp.concatenate([past_k, k.astype(past_k.dtype)], axis=1)
    v_all = jnp.concatenate([past_v, v.astype(past_v.dtype)], axis=1)
    o = diff_attend(q, k_all, v_all, past + jnp.arange(T), jnp.arange(past + T), lam, rel_bias)
    return diff_output(o, out_norm, lam_init, w_out), k, v

def setup_inputs(seed: int = 0) -> dict:
    key = jax.random.key(seed)
    keys = iter(jax.random.split(key, 64))
    f32 = jnp.float32

    def normal(shape, scale=1.0):
        return jax.random.normal(next(keys), shape, f32) * scale

    def gain(shape):
        return 1.0 + normal(shape, 0.02)

    n_pages = PAST_LEN // PAGE_SIZE
    n_used = DEC_BATCH * n_pages
    n_phys = n_used + max(1, n_used // 4)
    page_table = jax.random.permutation(next(keys), n_phys)[:n_used].reshape(DEC_BATCH, n_pages).astype(jnp.int32)
    dt0 = jnp.exp(jax.random.uniform(next(keys), (N_SSD, SSM_HEADS), f32, math.log(1e-3), math.log(1e-1)))
    dt_bias = dt0 + jnp.log(-jnp.expm1(-dt0))
    a_log = jnp.log(jax.random.uniform(next(keys), (N_SSD, SSM_HEADS), f32, 1.0, 16.0))
    swa_w = H_SWA = N_ATTN_HEADS * HEAD_DIM
    return {
        'x_prompt': normal((BATCH, SEQ, D_MODEL)),
        'x_sample': normal((DEC_BATCH, DEC_SEQ, D_MODEL)),
        'state_ssm_conv': normal((N_SSD, DEC_BATCH, CONV_W - 1, CONV_DIM)),
        'state_ssm': normal((N_SSD, DEC_BATCH, SSM_HEADS, SSM_HEAD_DIM, D_STATE), 0.1),
        'cache_swa_kv0': normal((N_SWA, DEC_BATCH, min(SWA_GROUPS[0][0], PAST_LEN), 2, SWA_HEADS_PER_GROUP, HEAD_DIM)),
        'cache_swa_kv1': normal((N_SWA, DEC_BATCH, min(SWA_GROUPS[1][0], PAST_LEN), 2, SWA_HEADS_PER_GROUP, HEAD_DIM)),
        'cache_swa_kv2': normal((N_SWA, DEC_BATCH, min(SWA_GROUPS[2][0], PAST_LEN), 2, SWA_HEADS_PER_GROUP, HEAD_DIM)),
        'cache_diff_k': normal((N_DIFF, n_phys, PAGE_SIZE, DIFF_KV_HEADS, 2, HEAD_DIM)),
        'cache_diff_v': normal((N_DIFF, n_phys, PAGE_SIZE, DIFF_KV_HEADS, DIFF_V_DIM)),
        'page_table': page_table,
        'rel_bias': normal((NUM_BUCKETS, N_ATTN_HEADS), 0.5),
        'norm_mix': gain((DEPTH, D_MODEL)),
        'norm_ffn': gain((DEPTH, D_MODEL)),
        'ffn_w_in': normal((DEPTH, D_MODEL, 2 * D_FF), D_MODEL ** -0.5),
        'ffn_w_out': normal((DEPTH, D_FF, D_MODEL), D_FF ** -0.5),
        'ssm_w_in': normal((N_SSD, D_MODEL, SSM_IN_DIM), D_MODEL ** -0.5),
        'ssm_conv_w': normal((N_SSD, CONV_W, CONV_DIM), CONV_W ** -0.5),
        'ssm_conv_b': normal((N_SSD, CONV_DIM), 0.02),
        'ssm_dt_bias': dt_bias,
        'ssm_a_log': a_log,
        'ssm_d': gain((N_SSD, SSM_HEADS)),
        'ssm_norm': gain((N_SSD, D_INNER)),
        'ssm_w_out': normal((N_SSD, D_INNER, D_MODEL), D_INNER ** -0.5),
        'swa_w_qkv': normal((N_SWA, D_MODEL, 3 * swa_w), D_MODEL ** -0.5),
        'swa_q_norm': gain((N_SWA, HEAD_DIM)),
        'swa_k_norm': gain((N_SWA, HEAD_DIM)),
        'swa_w_out': normal((N_SWA, H_SWA, D_MODEL), H_SWA ** -0.5),
        'diff_w_qkv': normal((N_DIFF, D_MODEL, DIFF_QKV_DIM), D_MODEL ** -0.5),
        'diff_q_norm': gain((N_DIFF, HEAD_DIM)),
        'diff_k_norm': gain((N_DIFF, HEAD_DIM)),
        'diff_lambda': normal((N_DIFF, 4, HEAD_DIM), 0.1),
        'diff_out_norm': gain((N_DIFF, DIFF_V_DIM)),
        'diff_w_out': normal((N_DIFF, N_ATTN_HEADS * DIFF_V_DIM, D_MODEL), (N_ATTN_HEADS * DIFF_V_DIM) ** -0.5),
    }

def reference(x_prompt, x_sample, state_ssm_conv, state_ssm, cache_swa_kv0, cache_swa_kv1, cache_swa_kv2,
              cache_diff_k, cache_diff_v, page_table, rel_bias, norm_mix, norm_ffn, ffn_w_in, ffn_w_out,
              ssm_w_in, ssm_conv_w, ssm_conv_b, ssm_dt_bias, ssm_a_log, ssm_d, ssm_norm, ssm_w_out,
              swa_w_qkv, swa_q_norm, swa_k_norm, swa_w_out,
              diff_w_qkv, diff_q_norm, diff_k_norm, diff_lambda, diff_out_norm, diff_w_out):
    xp, xs = x_prompt, x_sample
    bp = xp.shape[0]
    swa_caches = (cache_swa_kv0, cache_swa_kv1, cache_swa_kv2)
    conv_p, conv_s, ssm_p, ssm_s = [], [], [], []
    swa_p = tuple([] for _ in SWA_GROUPS)
    swa_s = tuple([] for _ in SWA_GROUPS)
    dk_p, dk_s, dv_p, dv_s = [], [], [], []
    i_ssd = i_swa = i_diff = 0
    for layer in range(DEPTH):
        hp = rmsnorm(xp, norm_mix[layer])
        hs = rmsnorm(xs, norm_mix[layer])
        kind = layer % N_MIXERS
        if kind == 0:
            i = i_ssd
            i_ssd += 1
            w = (ssm_w_in[i], ssm_conv_w[i], ssm_conv_b[i], ssm_dt_bias[i], ssm_a_log[i], ssm_d[i], ssm_norm[i], ssm_w_out[i])
            conv0 = jnp.zeros((bp, CONV_W - 1, CONV_DIM), hp.dtype)
            state0 = jnp.zeros((bp, SSM_HEADS, SSM_HEAD_DIM, D_STATE), jnp.float32)
            mp, c_p, s_p = ssd_mixer(hp, conv0, state0, *w)
            ms, c_s, s_s = ssd_mixer(hs, state_ssm_conv[i], state_ssm[i], *w)
            conv_p.append(c_p)
            conv_s.append(c_s)
            ssm_p.append(s_p)
            ssm_s.append(s_s)
        elif kind == 1:
            i = i_swa
            i_swa += 1
            w = (swa_w_qkv[i], swa_q_norm[i], swa_k_norm[i], swa_w_out[i], rel_bias)
            mp, bufs_p = swa_prompt(hp, *w)
            ms, bufs_s = swa_sample(hs, [c[i] for c in swa_caches], *w)
            for g in range(len(SWA_GROUPS)):
                swa_p[g].append(bufs_p[g])
                swa_s[g].append(bufs_s[g])
        else:
            i = i_diff
            i_diff += 1
            lam_init = 0.8 - 0.6 * math.exp(-0.3 * layer)
            w = (diff_w_qkv[i], diff_q_norm[i], diff_k_norm[i], diff_lambda[i], diff_out_norm[i], diff_w_out[i], rel_bias, lam_init)
            mp, k_p, v_p = diff_prompt(hp, *w)
            ms, k_s, v_s = diff_sample(hs, cache_diff_k[i], cache_diff_v[i], page_table, *w)
            dk_p.append(k_p)
            dk_s.append(k_s)
            dv_p.append(v_p)
            dv_s.append(v_s)
        xp = xp + mp.astype(xp.dtype)
        xs = xs + ms.astype(xs.dtype)
        xp = xp + swiglu(rmsnorm(xp, norm_ffn[layer]), ffn_w_in[layer], ffn_w_out[layer]).astype(xp.dtype)
        xs = xs + swiglu(rmsnorm(xs, norm_ffn[layer]), ffn_w_in[layer], ffn_w_out[layer]).astype(xs.dtype)
    ssm_conv_prompt = jnp.stack(conv_p)
    ssm_conv_sample = jnp.stack(conv_s)
    ssm_prompt = jnp.stack(ssm_p)
    ssm_sample = jnp.stack(ssm_s)
    swa_kv0_prompt = jnp.stack(swa_p[0])
    swa_kv0_sample = jnp.stack(swa_s[0])
    swa_kv1_prompt = jnp.stack(swa_p[1])
    swa_kv1_sample = jnp.stack(swa_s[1])
    swa_kv2_prompt = jnp.stack(swa_p[2])
    swa_kv2_sample = jnp.stack(swa_s[2])
    diff_k_prompt = jnp.stack(dk_p)
    diff_k_sample = jnp.stack(dk_s)
    diff_v_prompt = jnp.stack(dv_p)
    diff_v_sample = jnp.stack(dv_s)
    return (xp, xs, ssm_conv_prompt, ssm_conv_sample, ssm_prompt, ssm_sample,
            swa_kv0_prompt, swa_kv0_sample, swa_kv1_prompt, swa_kv1_sample, swa_kv2_prompt, swa_kv2_sample,
            diff_k_prompt, diff_k_sample, diff_v_prompt, diff_v_sample)


_drawn_inputs = setup_inputs


def setup_inputs(seed=0):
    import zlib

    import numpy as np

    out = dict(_drawn_inputs(seed))
    spreads = {}
    factors = {'ssm_d': 3.348,
     'swa_q_norm': 8.0,
     'swa_k_norm': 4.005,
     'diff_q_norm': 6.416,
     'diff_k_norm': 2.983,
     'diff_lambda': 8.0,
     'diff_out_norm': 19.563}
    for name, (base, spread) in spreads.items():
        noise = np.random.default_rng([zlib.crc32(name.encode()), seed]).standard_normal(out[name].shape)
        drawn = base * np.exp(spread * noise) if base else spread * noise
        out[name] = jnp.asarray(drawn.astype(out[name].dtype))
    for name, factor in factors.items():
        out[name] = (out[name] * factor).astype(out[name].dtype)
    return out
```

```python
import math
from contextlib import ExitStack, contextmanager

import numpy as np
import concourse.bass as bass
from concourse import mybir

F32 = mybir.dt.float32
F32R = mybir.dt.float32r
I32 = mybir.dt.int32
ALU = mybir.AluOpType
ACT = mybir.ActivationFunctionType
AX = mybir.AxisListType
ds = bass.ds

P = 128
D_MODEL = 1024
DEPTH = 4
SEQ = 256
NB, T = 8, 4
NS = NB * T
TOK = SEQ + NS
KD = D_MODEL // P
D_FF = 2816
KF = D_FF // P
SLOT = 16 * P
EPS = 1e-6
NEG = -1e30
PAST = 1024
PAGE = 128

D_INNER = 2048
CI = D_INNER // P
GROUPS = 4
N_STATE = 128
CONV_W = 4
CX = CI + 2 * GROUPS
CONV_DIM = CX * P
SSM_IN = D_INNER + CONV_DIM + 32
HEADS = 32
EXT = SEQ + CONV_W - 1 + NB * (T + CONV_W - 1)
EXTS = SEQ + CONV_W - 1
NH = 12
HD = 64
WINDOWS = ((128, 1), (512, 4), (2048, 16))
GH = 4
SWA_C = 6
KVH, REP = 4, 3
QD_C = 12
LAM_INIT = 0.8 - 0.6 * math.exp(-0.3 * 2)

C_ID, C_ONE, C_BLK, C_ANTI, C_TRI, C_TRIS, C_SAME, C_BCOL, C_COMB, C_END = (
    0, 128, 256, 384, 512, 640, 768, 896, 904, 1000)
V_MIX, V_FFN, V_SSM, V_DOUT, V_QK, V_CONV = 0, 32, 64, 96, 97, 128


class Signal:
    times = 1
    every = []

    def __init__(self, nc, name, step=1):
        self.sem, self.step, self.base, self.seen = nc.alloc_semaphore(name), step, 0, 0
        Signal.every.append(self)

    def inc(self):
        self.seen += self.step * Signal.times
        return self.step

    def at(self, n):
        return n * self.step + self.base


@contextmanager
def repeat(eng, n):
    before = Signal.times
    Signal.times = before * n
    with eng.Fori(0, n) as i:
        yield i
    Signal.times = before


def pairs(eng, lo, hi, step, body):
    n = (hi - lo) // step
    if n > 1:
        with repeat(eng, n) as it:
            for r in range(step):
                body(it * step + (lo + r), (lo + r) % step)
    else:
        n = 0
    for i in range(lo + n * step, hi):
        body(i, i % step)


class Linear:
    def __init__(self, n, kk, jj, loads, step=2, cols=P):
        self.n, self.kk, self.jj, self.loads, self.step, self.cols = n, kk, jj, loads, step, cols
        self.width = kk * jj * cols


def columns(w, kk, jj, cols=P, col0=0):
    wv, n, h = w.rearrange("(k p) n -> p k n", p=P), jj * cols, kk // 2

    def loads(i, r, slot):
        v = slot[:, 0:kk * n].rearrange("p (k n) -> p k n", n=n)
        return [(v[:, a:b, :], wv[:, a:b, ds(i * n + col0, n)]) for a, b in ((0, h), (h, kk))]
    return loads


def gate_up(w):
    wv = w.rearrange("(k p) n -> p k n", p=P)

    def loads(i, r, slot):
        v = slot.rearrange("p (k j n) -> p k j n", j=2, n=P)
        return [(v[:, :, j, :], wv[:, :, ds(i * P + j * D_FF, P)]) for j in range(2)]
    return loads


def down_halves(w):
    wv, kk = w.rearrange("(k p) n -> p k n", p=P), KF // 2

    def loads(i, r, slot):
        h = r % 2
        v = slot[:, 0:kk * P].rearrange("p (k n) -> p k n", n=P)
        cut = kk // 2
        return [(v[:, a:b, :], wv[:, h * kk + a:h * kk + b, ds((i - h) * (P // 2), P)])
                for a, b in ((0, cut), (cut, kk))]
    return loads


def build_program(nc, A, O, order=None):
    Signal.every, Signal.times = [], 1
    stack = ExitStack()
    sig = {}

    def S(name, step=1):
        if name not in sig:
            sig[name] = Signal(nc, name, step)
        return sig[name]

    uid = [0]

    @contextmanager
    def phase():
        uid[0] += 1
        with ExitStack() as mem:
            def sb(name, shape, dt=F32):
                return mem.enter_context(nc.sbuf_tensor(f"{name}_{uid[0]}", shape, dt))
            with nc.Block() as block:
                yield block, sb
            for s in Signal.every:
                s.base += s.seen
                s.seen = 0

    def sb0(name, shape, dt=F32):
        return stack.enter_context(nc.sbuf_tensor(name, shape, dt))

    cst = sb0("cst", [P, C_END])
    vec = sb0("vec", [P, 3, P])
    perhead = sb0("perhead", [HEADS, 3, 2])
    lamcol = sb0("lamcol", [P, 1])
    x = sb0("x", [P, KD, TOK])
    raw = sb0("raw", [P, 2, SLOT])
    ps = stack.enter_context(nc.psum_tensor("ps", [P, 8, 512], F32))
    ident, ones, blk64 = (cst[:, c:c + P] for c in (C_ID, C_ONE, C_BLK))

    stream = dict(next=0)
    raw_loaded = [S(f"raw_loaded{s}", 16) for s in range(2)]
    hi_ready, lo_ready, blocks_done = S("weights_hi_ready"), S("weights_lo_ready"), S("blocks_done")

    def load_block(sp, lin, i, r, g, slot, wait=True):
        if wait:
            sp.wait_ge(lo_ready.sem, g - 1)
        for dst, src in lin.loads(i, r, raw[:, slot, :]):
            sp.dma_start(dst, src).then_inc(raw_loaded[slot].sem, raw_loaded[slot].inc())

    def linear_phase(segs, nxt, source=None, norm=None):
        b0 = stream["next"]
        total = sum(lin.n for lin, _ in segs)
        stream["next"] = b0 + total
        kin = KD if norm is not None else segs[0][0].kk
        with phase() as (block, sb):
            wh, wl = sb("wh", [P, 2, SLOT], F32R), sb("wl", [P, 2, SLOT], F32R)
            ah, al = sb("ah", [P, kin, TOK], F32R), sb("al", [P, kin, TOK], F32R)
            act_hi, act_lo = S("act_hi"), S("act_lo")
            sq_ready, sumsq, mean_ready, rstd_ready, normed = (
                S(n) for n in ("sq_ready", "sumsq", "mean_ready", "rstd_ready", "normed"))
            if norm is not None:
                sq, hn, rs = sb("sq", [P, KD, TOK]), sb("hn", [P, KD, TOK]), sb("rs", [P, 3, TOK])
            evacs = [e(sb, (ah, al, act_lo)) for _, e in segs]
            bases = [sum(l.n for l, _ in segs[:n]) for n in range(len(segs))]

            @block.sync
            def _(sp):
                for (lin, _), base in zip(segs, bases):
                    pairs(sp, 0 if base else 2, lin.n, 2, lambda i, r: load_block(
                        sp, lin, i, r, b0 + base + i, (b0 + base + r) % 2))
                for i in range(2 if nxt else 0):
                    load_block(sp, nxt, i, i, b0 + total + i, (b0 + total + i) % 2)

            def split_hi(act, g, s, width, free):
                act.wait_ge(raw_loaded[s].sem, (g - s) * 16 + 32)
                if free:
                    act.wait_ge(blocks_done.sem, g - 1)
                act.activation(wh[:, s, 0:width], raw[:, s, 0:width], ACT.Copy).then_inc(hi_ready.sem, hi_ready.inc())

            def split_lo(dve, g, s, width, free):
                dve.wait_ge(hi_ready.sem, g + 1)
                if free:
                    dve.wait_ge(blocks_done.sem, g - 1)
                dve.tensor_tensor(wl[:, s, 0:width], raw[:, s, 0:width],
                                  wh[:, s, 0:width].bitcast(F32), ALU.subtract).then_inc(lo_ready.sem, lo_ready.inc())

            def width_of(place):
                found = [lin.width for (lin, _), b in zip(segs, bases) if b <= place < b + lin.n]
                return found[0] if found else 0

            def blocks_of(eng, split, who):
                for n, (lin, _) in enumerate(segs):
                    before, after = evacs[n].get(who, (None, None))

                    def body(i, r, ahead=lin.width):
                        if before:
                            before(eng, i, r, b0 + bases[n] + i)
                        if ahead:
                            split(eng, b0 + bases[n] + i + 2, (b0 + bases[n] + r) % 2, ahead, True)
                        if after:
                            after(eng, i, r, b0 + bases[n] + i)
                    whole = max(0, lin.n - 2) // lin.step * lin.step
                    pairs(eng, 0, whole, lin.step, body)
                    for i in range(whole, lin.n):
                        body(i, i % lin.step, width_of(bases[n] + i + 2))

            @block.scalar
            def _(act):
                for i in range(2):
                    split_hi(act, b0 + i, (b0 + i) % 2, segs[0][0].width, False)
                if norm is not None:
                    for c in range(KD):
                        act.activation(sq[:, c, :], x[:, c, :], ACT.Square).then_inc(sq_ready.sem, sq_ready.inc())
                    act.wait_ge(mean_ready.sem, mean_ready.at(1))
                    act.activation(rs[:, 1, :], rs[:, 0, :], ACT.Ln).then_inc(rstd_ready.sem, rstd_ready.inc())
                    act.wait_ge(rstd_ready.sem, rstd_ready.at(1))
                    act.activation(rs[:, 2, :], rs[:, 1, :], ACT.Exp, scale=-0.5).then_inc(
                        rstd_ready.sem, rstd_ready.inc())
                for c in range(kin):
                    if norm is not None:
                        act.wait_ge(normed.sem, normed.at(c + 1))
                    act.activation(ah[:, c, :], hn[:, c, :] if norm is not None else source(c),
                                   ACT.Copy).then_inc(act_hi.sem, act_hi.inc())
                blocks_of(act, split_hi, "act")

            @block.vector
            def _(dve):
                for i in range(2):
                    split_lo(dve, b0 + i, (b0 + i) % 2, segs[0][0].width, False)
                if norm is not None:
                    dve.wait_ge(sumsq.sem, sumsq.at(1))
                    dve.tensor_scalar(rs[:, 0, :], ps[:, 7, 0:TOK], 1.0 / D_MODEL, EPS,
                                      ALU.mult, ALU.add).then_inc(mean_ready.sem, mean_ready.inc())
                    dve.wait_ge(rstd_ready.sem, rstd_ready.at(2))
                for c in range(kin + 1):
                    if norm is not None and c < kin:
                        dve.scalar_tensor_tensor(
                            out=hn[:, c, :], in0=x[:, c, :], scalar=vec[:, 0, norm + c:norm + c + 1],
                            in1=rs[:, 2, :], op0=ALU.mult, op1=ALU.mult).then_inc(normed.sem, normed.inc())
                    if c >= 1:
                        dve.wait_ge(act_hi.sem, act_hi.at(c))
                        if norm is not None:
                            dve.wait_ge(normed.sem, normed.at(c))
                        dve.tensor_tensor(
                            al[:, c - 1, :], hn[:, c - 1, :] if norm is not None else source(c - 1),
                            ah[:, c - 1, :].bitcast(F32), ALU.subtract).then_inc(act_lo.sem, act_lo.inc())
                blocks_of(dve, split_lo, "dve")

            @block.tensor
            def _(pe):
                if norm is not None:
                    for c in range(KD):
                        pe.wait_ge(sq_ready.sem, sq_ready.at(c + 1))
                        mm = pe.matmul(ps[:, 7, 0:TOK], ones, sq[:, c, :], start=(c == 0), stop=(c == KD - 1))
                    mm.then_inc(sumsq.sem, sumsq.inc())
                for n, (lin, _) in enumerate(segs):
                    def body(i, r):
                        g, s = b0 + bases[n] + i, (b0 + bases[n] + r) % 2
                        W = [w[:, s, 0:lin.width].rearrange("p (k j n) -> p k j n", k=lin.kk, j=lin.jj)
                             for w in (wh, wl)]
                        outs, ks, first, last, (xh, xl, ready), freed = evacs[n]["plan"](i, r, bases[n])
                        if freed is not None:
                            pe.wait_ge(freed[0].sem, freed[1])
                        pe.wait_ge(hi_ready.sem, g + 1)
                        for kk, k in enumerate(ks):
                            pe.wait_ge(ready.sem, ready.at(k + 1))
                            for j, out in enumerate(outs):
                                for part in (xh, xl):
                                    pe.matmul(out, W[0][:, kk, j, :], part[:, k, :], stop=False,
                                              start=(first and kk == 0 and part is xh), skip_group_check=True)
                        pe.wait_ge(lo_ready.sem, g + 1)
                        for kk, k in enumerate(ks):
                            for j, out in enumerate(outs):
                                mm = pe.matmul(out, W[1][:, kk, j, :], xh[:, k, :], start=False,
                                               stop=(last and kk == len(ks) - 1), skip_group_check=True)
                        mm.then_inc(blocks_done.sem, blocks_done.inc())
                    pairs(pe, 0, lin.n, lin.step, body)

            if any("pool" in e for e in evacs):
                @block.gpsimd
                def _(pool):
                    for e in evacs:
                        if "pool_start" in e:
                            e["pool_start"](pool)
                    for n, (lin, _) in enumerate(segs):
                        if "pool" in evacs[n]:
                            pairs(pool, 0, lin.n, lin.step, lambda i, r: evacs[n]["pool"](pool, i, r, b0 + bases[n] + i))


    out_read, down_read = S("out_read"), S("down_read", 2)

    def bank_of(b, r):
        return 2 * ((b + r) % 2)

    def two_banks(parts, ks, count=2):
        def plan(i, r, b):
            outs = [ps[:, bank_of(b, r) + j, 0:TOK] for j in range(count)]
            return outs, ks, True, True, parts, (out_read, out_read.at(b + i - 1))
        return plan

    def ffn_up(sb, parts, shared):
        sg, gh = sb("sg", [P, 2, TOK]), sb("gh", [P, 2, TOK])
        hh, hl = sb("hh", [P, KF, TOK], F32R), sb("hl", [P, KF, TOK], F32R)
        silu_ready, hid_hi, hid_lo = S("silu_ready"), S("hidden_hi"), S("hidden_lo")
        shared["hidden"] = (hh, hl, hid_lo)

        def act_before(act, i, r, g):
            act.wait_ge(blocks_done.sem, g + 1)
            act.wait_ge(out_read.sem, out_read.at(i - 1))
            act.activation(sg[:, r, :], ps[:, 2 * r, 0:TOK], ACT.Silu).then_inc(silu_ready.sem, silu_ready.inc())

        def dve_before(dve, i, r, g):
            dve.wait_ge(silu_ready.sem, silu_ready.at(i + 1))
            dve.wait_ge(hid_lo.sem, hid_lo.at(i - 1))
            dve.tensor_tensor(gh[:, r, :], ps[:, 2 * r + 1, 0:TOK], sg[:, r, :], ALU.mult).then_inc(
                out_read.sem, out_read.inc())

        def act_after(act, i, r, g):
            act.wait_ge(out_read.sem, out_read.at(i + 1))
            act.activation(hh[:, ds(i, 1), :], gh[:, r:r + 1, :], ACT.Copy).then_inc(hid_hi.sem, hid_hi.inc())

        def dve_after(dve, i, r, g):
            dve.wait_ge(hid_hi.sem, hid_hi.at(i + 1))
            dve.tensor_tensor(hl[:, ds(i, 1), :], gh[:, r:r + 1, :],
                              hh[:, ds(i, 1), :].bitcast(F32), ALU.subtract).then_inc(hid_lo.sem, hid_lo.inc())
        return dict(plan=two_banks(parts, range(KD)), act=(act_before, act_after), dve=(dve_before, dve_after))

    copied = S("cache_copied", 16)

    def kept_rows(layer):
        pick = lambda g, src, dst, n: (A[f"cache_swa_kv{g}"], O[f"swa_kv{g}_sample"], src, dst, n)
        return ([pick(0, T, 0, WINDOWS[0][0] - T), pick(1, T, 0, WINDOWS[1][0] - T)],
                [pick(2, 0, 0, PAST // 2)], [pick(2, PAST // 2, PAST // 2, PAST // 2)], [])[layer]

    def ffn_down(sb, parts, shared, layer):
        def plan(i, r, b):
            h = r % 2
            freed = None if h else (down_read, down_read.base + i - 2)
            return ([ps[:, 4 + r // 2, 0:TOK]], range(h * (KF // 2), (h + 1) * (KF // 2)), h == 0, h == 1,
                    shared["hidden"], freed)

        def dve_before(dve, i, r, g):
            if r % 2:
                dve.wait_ge(blocks_done.sem, g + 1)
                xc = x.rearrange("p k n -> p (k n)")[:, ds((i - 1) * (TOK // 2), TOK)]
                dve.tensor_tensor(xc, xc, ps[:, 4 + r // 2, 0:TOK], ALU.add).then_inc(down_read.sem, down_read.inc())

        def act_copy(act, i, r, g):
            for src, dst, a, b, n in kept_rows(layer) if r % 2 else ():
                views = []
                for cache, row in ((src, a), (dst, b)):
                    size = cache.shape[2] * cache.shape[3] * GH * HD
                    flat = cache.rearrange("l b w k h d -> (l b w k h d)")
                    views.append(flat[ds((i - 1) * (size // 2) + row * 2 * GH * HD, n * 2 * GH * HD)].rearrange(
                        "(w n) -> w n", n=2 * GH * HD))
                act.dma_start(views[1], views[0]).then_inc(copied.sem, copied.inc())
        return dict(plan=plan, act=(act_copy, None), dve=(dve_before, None))

    def ffn_first(layer):
        return Linear(KF, KD, 2, gate_up(A["ffn_w_in"][layer]))

    def ffn(layer, nxt):
        shared = {}
        down = Linear(2 * KD, KF // 2, 1, down_halves(A["ffn_w_out"][layer]), step=4)
        linear_phase([(ffn_first(layer), lambda sb, parts: ffn_up(sb, parts, shared)),
                      (down, lambda sb, parts: ffn_down(sb, parts, shared, layer))], nxt, norm=V_FFN + layer * KD)

    dist_tab = nc.dram_tensor("dist_tab", (4, NH, 512), F32, kind="Internal").ap()

    loaded = S("loaded", 16)
    turned, moved, made = S("turned"), S("moved"), S("made")
    made2, tab_made, tab_moved, tab_stored = S("row_filled"), S("tables_made"), S("tables_moved"), S("table_stored", 16)

    LEADS = dict(out_read=2, down_read=2, hidden_lo=2, conv_ready=2, tail_ready=3, state_moved=2, state_updated=5,
                 y_state=2, state_outer=5, old_scored=2, probs_turned=2, pv=2,
                 keys_moved_act=2, keys_moved_dve=2)

    def setup(nxt):
        with phase() as (block, sb):
            rows = sb("rows", [P, 3, P])
            xt = sb("xt", [P, 3, D_MODEL])
            lam = sb("lam", [1, 4, HD])
            lw = sb("lw", [1, 2 * HD + 8])
            scratch = sb("scratch", [1, 64])
            oh, rb, tab = sb("oh", [33, 4, 512]), sb("rb", [33, NH]), sb("tab", [NH, 4, 512])
            groups = [[], [], []]
            v128 = lambda ap: ap.rearrange("l (k n) -> (l k) n", n=P)
            groups[0] = [(cst[:, :], A["constants"]),
                         (rows[V_MIX:V_MIX + 32, 0, :], v128(A["norm_mix"])),
                         (rows[V_FFN:V_FFN + 32, 0, :], v128(A["norm_ffn"])),
                         (rows[V_SSM:V_SSM + 32, 0, :], v128(A["ssm_norm"])),
                         (rows[V_DOUT:V_DOUT + 1, 0, :], A["diff_out_norm"])]
            for n, name in enumerate(("swa_q_norm", "swa_k_norm", "diff_q_norm", "diff_k_norm")):
                for half in range(2):
                    groups[0].append((rows[V_QK + n:V_QK + n + 1, 0, half * HD:(half + 1) * HD], A[name]))
            for l in range(2):
                groups[0].append((rows[0:CONV_W * CX, 1 + l, :],
                                  A["ssm_conv_w"][l].rearrange("w (k n) -> (w k) n", n=P)))
                groups[0].append((rows[CONV_W * CX:(CONV_W + 1) * CX, 1 + l, :],
                                  A["ssm_conv_b"][l:l + 1, :].rearrange("l (k n) -> (l k) n", n=P)))
            groups[0] += [(xt[:, t, :], A["x_prompt"][0, t * P:(t + 1) * P, :]) for t in range(2)]
            groups[0].append((xt[0:NS, 2, :], A["x_sample"].rearrange("b t d -> (b t) d")))
            for n, name in enumerate(("ssm_dt_bias", "ssm_a_log", "ssm_d")):
                for l in range(2):
                    groups[0].append((perhead[:, n, l:l + 1], A[name][l:l + 1, :].rearrange("l h -> h l")))
            groups[0].append((lam[:, :, :], A["diff_lambda"]))
            groups[0] += [(oh[:, :, :], A["onehot_dist"]), (rb[0:32, :], A["rel_bias"])]
            used = (V_QK + 4, (CONV_W + 1) * CX, (CONV_W + 1) * CX)

            @block.sync
            def _(sp):
                for dst, src in groups[0]:
                    sp.dma_start(dst, src).then_inc(loaded.sem, loaded.inc())
                for i in range(2):
                    load_block(sp, nxt, i, i, i, i, wait=False)
                sp.wait_ge(tab_moved.sem, tab_moved.at(4))
                sp.dma_start(dist_tab.rearrange("k h n -> h k n"), tab[:, :, :]).then_inc(
                    tab_stored.sem, tab_stored.inc())
                sp.wait_ge(tab_stored.sem, tab_stored.at(1))

            @block.gpsimd
            def _(pool):
                n = 0
                for name, lead in LEADS.items():
                    for _ in range(lead):
                        pool.memset(scratch[:, n:n + 1], 0.0).then_inc(S(name).sem, S(name).inc())
                        n += 1

            @block.tensor
            def _(pe):
                pe.wait_ge(loaded.sem, loaded.at(len(groups[0])))
                for n in range(3):
                    pe.transpose(ps[:, n, 0:used[n]], rows[0:used[n], n, :],
                                 ident[0:used[n], 0:used[n]]).then_inc(turned.sem, turned.inc())
                for c in range(KD):
                    if c >= 4:
                        pe.wait_ge(moved.sem, moved.at(3 + c - 4 + 1))
                    for t, n in ((0, P), (1, P), (2, NS)):
                        mm = pe.transpose(ps[:, 3 + c % 4, t * P:t * P + n], xt[0:n, t, c * P:(c + 1) * P],
                                          ident[0:n, 0:n])
                    mm.then_inc(turned.sem, turned.inc())
                pe.wait_ge(made2.sem, made2.at(1))
                for k in range(4):
                    if k < 3:
                        pe.wait_ge(moved.sem, moved.at(k + 1))
                    else:
                        pe.wait_ge(moved.sem, moved.at(3 + 5))
                    pe.matmul(ps[0:NH, k, :], rb[:, :], oh[:, k, :], start=True, stop=True).then_inc(
                        tab_made.sem, tab_made.inc())
                pe.wait_ge(made.sem, made.at(4))
                pe.matmul(ps[:, 7, 0:1], ones[0:1, :], lw[:, 2 * HD + 4:2 * HD + 5],
                          start=True, stop=True).then_inc(turned.sem, turned.inc())

            @block.scalar
            def _(act):
                act.wait_ge(made.sem, made.at(2))
                act.activation(lw[:, 2 * HD + 2:2 * HD + 4], lw[:, 2 * HD:2 * HD + 2], ACT.Exp).then_inc(
                    made.sem, made.inc())

            @block.vector
            def _(dve):
                dve.memset(rb[32:33, :], NEG).then_inc(made2.sem, made2.inc())
                for n in range(3):
                    dve.wait_ge(turned.sem, turned.at(n + 1))
                    dve.tensor_copy(vec[:, n, 0:used[n]], ps[:, n, 0:used[n]]).then_inc(moved.sem, moved.inc())
                for c in range(KD):
                    dve.wait_ge(turned.sem, turned.at(3 + c + 1))
                    dve.tensor_copy(x[:, c, :], ps[:, 3 + c % 4, 0:TOK]).then_inc(moved.sem, moved.inc())
                for k in range(4):
                    dve.wait_ge(tab_made.sem, tab_made.at(k + 1))
                    dve.tensor_copy(tab[:, k, :], ps[0:NH, k, :]).then_inc(tab_moved.sem, tab_moved.inc())
                dve.tensor_tensor(lw[:, 0:2 * HD].rearrange("p (a n) -> p a n", a=2),
                                  lam[:, 0:4:2, :], lam[:, 1:4:2, :], ALU.mult).then_inc(made.sem, made.inc())
                dve.wait_ge(made.sem, made.at(1))
                dve.tensor_reduce(lw[:, 2 * HD:2 * HD + 2],
                                  lw[:, 0:2 * HD].rearrange("p (a n) -> p a n", a=2), AX.X, ALU.add).then_inc(
                    made.sem, made.inc())
                dve.wait_ge(made.sem, made.at(3))
                dve.scalar_tensor_tensor(
                    out=lw[:, 2 * HD + 4:2 * HD + 5], in0=lw[:, 2 * HD + 3:2 * HD + 4], scalar=-LAM_INIT,
                    in1=lw[:, 2 * HD + 2:2 * HD + 3], op0=ALU.add, op1=ALU.subtract).then_inc(made.sem, made.inc())
                dve.wait_ge(turned.sem, turned.at(3 + KD + 1))
                dve.tensor_copy(lamcol[:, :], ps[:, 7, 0:1]).then_inc(moved.sem, moved.inc())

    def finish():
        stored = S("stored", 16)
        with phase() as (block, sb):
            yt = sb("yt", [P, 3, D_MODEL])
            tiles = ((0, P), (1, P), (2, NS))

            @block.tensor
            def _(pe):
                for t, n in tiles:
                    for h in range(2):
                        for c in range(4):
                            mm = pe.transpose(ps[0:n, 2 * t + h, c * P:(c + 1) * P],
                                              x[:, 4 * h + c, t * P:t * P + n], ident)
                        mm.then_inc(turned.sem, turned.inc())

            @block.vector
            def _(dve):
                for t, n in tiles:
                    for h in range(2):
                        dve.wait_ge(turned.sem, turned.at(2 * t + h + 1))
                        dve.tensor_copy(yt[0:n, t, h * 512:(h + 1) * 512], ps[0:n, 2 * t + h, :]).then_inc(
                            moved.sem, moved.inc())

            @block.sync
            def _(sp):
                for t, n in tiles:
                    sp.wait_ge(moved.sem, moved.at(2 * t + 2))
                    dst = O["y_prompt"][0, t * P:(t + 1) * P, :] if t < 2 else \
                        O["y_sample"].rearrange("b t d -> (b t) d")
                    sp.dma_start(dst, yt[0:n, t, :]).then_inc(stored.sem, stored.inc())
                sp.wait_ge(stored.sem, stored.at(3))
                sp.wait_ge(copied.sem, copied.base)

    TILES = ((0, P), (1, P), (2, NS))

    def cols_of(t):
        return slice(t * P, t * P + (NS if t == 2 else P))

    def residual(sb, parts, kk):
        def dve_before(dve, i, r, g):
            dve.wait_ge(blocks_done.sem, g + 1)
            xc = x.rearrange("p k n -> p (k n)")[:, ds(i * TOK, TOK)]
            dve.tensor_tensor(xc, xc, ps[:, 2 * (r % 2), 0:TOK], ALU.add).then_inc(out_read.sem, out_read.inc())
        return dict(plan=two_banks(parts, range(kk), 1), dve=(dve_before, None))

    def ssd_first(layer):
        return Linear(CI // 2, KD, 2, columns(A["ssm_w_in"][layer // 3], KD, 2))

    def ssd(layer, nxt):
        i_ssd = layer // 3
        w = A["ssm_w_in"][i_ssd]
        vconv = lambda tap, c: vec[:, 1 + i_ssd, tap * CX + c:tap * CX + c + 1]
        mem = ExitStack()
        m = {}

        def keep(name, shape, dt=F32):
            m[name] = mem.enter_context(nc.sbuf_tensor(f"{name}_L{layer}", shape, dt))
            return m[name]

        Z, XB = keep("Z", [P, CI, TOK]), keep("XB", [P, CX, TOK])
        dtT = keep("dtT", [HEADS, TOK])
        early = ExitStack()
        tail = keep("tail", [P, CX, 1 + NB, 3])
        stT = early.enter_context(nc.sbuf_tensor(f"stT_L{layer}", [P, CX, NB, 3], F32))

        with phase() as (block, sb):
            strow = sb("strow", [NB * 3, CONV_DIM])

            @block.sync
            def _(sp):
                sp.dma_start(strow[:, :], A["state_ssm_conv"][i_ssd].rearrange("b w n -> (b w) n")).then_inc(
                    loaded.sem, loaded.inc())

            @block.tensor
            def _(pe):
                pe.wait_ge(loaded.sem, loaded.at(1))
                for c in range(CX):
                    mm = pe.transpose(ps[:, c // 12, (c % 12) * 24:(c % 12) * 24 + 24],
                                      strow[:, c * P:(c + 1) * P], ident[0:24, 0:24])
                mm.then_inc(turned.sem, turned.inc())

            @block.vector
            def _(dve):
                dve.wait_ge(turned.sem, turned.at(1))
                dve.tensor_copy(stT.rearrange("p (a c) b w -> p a (c b w)", a=2), ps[:, 0:2, 0:288]).then_inc(
                    moved.sem, moved.inc())

        state_in, tap_done, conv_ready, tail_ready, first_tap = (
            S(n) for n in ("state_in", "tap_done", "conv_ready", "tail_ready", "first_tap"))

        def z_evac(sb, parts):
            def act_before(act, i, r, g):
                act.wait_ge(blocks_done.sem, g + 1)
                act.activation(Z[:, ds(2 * i, 2), :], ps[:, 2 * r:2 * r + 2, 0:TOK], ACT.Silu).then_inc(
                    out_read.sem, out_read.inc())
            return dict(plan=two_banks(parts, range(KD)), act=(act_before, None))

        def xbc_evac(sb, parts):
            ext, cv = sb("ext", [P, 2, 2, EXT]), sb("cv", [P, 2, 2, EXT])
            samples = lambda t, r: t[:, r, :, EXTS:EXT].rearrange("p j (b w) -> p j b w", b=NB)
            n0 = CI // 2

            def act_before(act, i, r, g):
                act.wait_ge(blocks_done.sem, g + 1)
                act.wait_ge(conv_ready.sem, conv_ready.at(i - 1))
                act.wait_ge(tail_ready.sem, tail_ready.at(2 * i - 2))
                b = 2 * r
                act.activation(ext[:, r, :, 3:3 + SEQ], ps[:, b:b + 2, 0:SEQ], ACT.Copy).then_inc(
                    first_tap.sem, first_tap.inc())
                act.activation(samples(ext, r)[:, :, :, 3:3 + T],
                               ps[:, b:b + 2, SEQ:TOK].rearrange("p j (b t) -> p j b t", b=NB),
                               ACT.Copy).then_inc(out_read.sem, out_read.inc())
                act.wait_ge(out_read.sem, out_read.at(n0 + i + 1))
                act.wait_ge(state_in.sem, state_in.at(i + 1))
                for j in range(2):
                    act.activation(cv[:, r, j, 0:EXT - 3], ext[:, r, j, 0:EXT - 3], ACT.Identity,
                                   scale=convw(0, i, j), bias=convw(CONV_W, i, j)).then_inc(
                        first_tap.sem, first_tap.inc())

            def convw(tap, i, j):
                return vec[:, 1 + i_ssd, ds(2 * i + (tap * CX + j), 1)]

            def dve_before(dve, i, r, g):
                n = 0
                for tap in range(1, CONV_W):
                    for j in range(2):
                        if tap == 1:
                            dve.wait_ge(first_tap.sem, first_tap.at(3 * i + 2 + j))
                        else:
                            dve.wait_ge(tap_done.sem, tap_done.at(6 * i + (n - 1)))
                        dve.scalar_tensor_tensor(
                            out=cv[:, r, j, 0:EXT - 3], in0=ext[:, r, j, tap:EXT - 3 + tap],
                            scalar=convw(tap, i, j), in1=cv[:, r, j, 0:EXT - 3], op0=ALU.mult, op1=ALU.add).then_inc(
                            tap_done.sem, tap_done.inc())
                        n += 1

            def act_after(act, i, r, g):
                act.wait_ge(tap_done.sem, tap_done.at(6 * i + 6))
                act.activation(XB[:, ds(2 * i, 2), 0:SEQ], cv[:, r, :, 0:SEQ], ACT.Silu).then_inc(
                    conv_read.sem, conv_read.inc())
                act.activation(
                    XB[:, ds(2 * i, 2), SEQ:TOK].rearrange("p j (b t) -> p j b t", b=NB),
                    samples(cv, r)[:, :, :, 0:T], ACT.Silu).then_inc(conv_ready.sem, conv_ready.inc())
            conv_read = S("conv_prompt_ready")

            def pool_all(pl, i, r, g):
                pl.wait_ge(conv_ready.sem, conv_ready.at(i - 1))
                pl.tensor_copy(samples(ext, r)[:, :, :, 0:3], stT[:, ds(2 * i, 2), :, :]).then_inc(
                    state_in.sem, state_in.inc())
                pl.wait_ge(out_read.sem, out_read.at(n0 + i + 1))
                pl.tensor_copy(tail[:, ds(2 * i, 2), 0, :], ext[:, r, :, SEQ:SEQ + 3]).then_inc(
                    tail_ready.sem, tail_ready.inc())
                pl.tensor_copy(tail[:, ds(2 * i, 2), 1:1 + NB, :], samples(ext, r)[:, :, :, T:T + 3]).then_inc(
                    tail_ready.sem, tail_ready.inc())
            zeroed = S("ext_zeroed")

            def pool_start(pl):
                pl.memset(ext[:, :, :, 0:3], 0.0).then_inc(zeroed.sem, zeroed.inc())
            return dict(plan=two_banks(parts, range(KD)), act=(act_before, act_after), dve=(dve_before, None),
                        pool=pool_all, pool_start=pool_start)

        def dt_evac(sb, parts):
            def act_before(act, i, r, g):
                act.wait_ge(blocks_done.sem, g + 1)
                act.activation(dtT[:, :], ps[96:128, 0, 0:TOK], ACT.Copy).then_inc(out_read.sem, out_read.inc())
            return dict(plan=two_banks(parts, range(KD), 1), act=(act_before, None))

        linear_phase([
            (ssd_first(layer), z_evac),
            (Linear(CX // 2, KD, 2, columns(w, KD, 2, col0=D_INNER)), xbc_evac),
            (Linear(1, KD, 1, columns(w, KD, 1, col0=SSM_IN - P)), dt_evac)],
            Linear(KD, CI, 1, columns(A["ssm_w_out"][i_ssd], CI, 1)), norm=V_MIX + layer * KD)
        early.close()

        dtk, adk = keep("dtk", [P, 3, HEADS]), keep("adk", [P, 3, HEADS])
        ack, acT = keep("ack", [P, 3, HEADS]), keep("acT", [HEADS, TOK])
        EA, dsk = keep("EA", [P, CI, NS]), keep("dsk", [P, CI])
        XD, Bt = keep("XD", [P, 3, D_INNER]), keep("Bt", [P, 3, GROUPS * N_STATE])
        U2, S0 = keep("U2", [NS, D_INNER]), keep("S0", [P, D_INNER])
        cbm, yS = keep("cbm", [P, GROUPS, TOK]), keep("yS", [P, CI, NS])
        heads_of = lambda ap: ap.rearrange("p (h n) -> p h n", n=64)
        soft, softe, adt_ready, small, smalls, decays, expand, expanded = (
            S(n) for n in ("softplus", "softplus_exp", "adt_ready", "token_sums", "token_sums_read",
                           "decay_args", "expand", "expanded"))
        dec_ready, x_turned, x_moved, b_moved, scaled, state_mm, states_out, cb_mm, cb_ready = (
            S(n) for n in ("decays", "x_turned", "x_moved", "b_moved", "scaled", "state_sums",
                           "states_moved", "cb_products", "cb_masked"))
        stored, cleared = S("stored", 16), S("cleared")
        with phase() as (block, sb):
            sp_ = sb("sp", [HEADS, 8, TOK])
            ea = sb("ea", [HEADS, 1])
            adT = sb("adT", [HEADS, TOK])
            tot, arg, dec = sb("tot", [P, 3, HEADS]), sb("arg", [P, 4, HEADS]), sb("dec", [P, 4, HEADS])
            U, Fs, tl = sb("U", [P, 3, D_INNER]), sb("Fs", [P, D_INNER]), sb("tl", [27, CONV_DIM])
            tri, tris, same = (cst[:, c:c + P] for c in (C_TRI, C_TRIS, C_SAME))
            dt_bias, a_log = perhead[:, 0, i_ssd:i_ssd + 1], perhead[:, 1, i_ssd:i_ssd + 1]
            v, av, e, s, s2, p, mx, t_ = (sp_[:, n, :] for n in range(8))

            @block.gpsimd
            def _(pool):
                pool.memset(cbm[:, :, SEQ:TOK], 0.0).then_inc(cleared.sem, cleared.inc())

            @block.vector
            def _(dve):
                n = 0

                def step(ins):
                    nonlocal n
                    ins.then_inc(soft.sem, soft.inc())
                    n += 1
                    dve.wait_ge(soft.sem, soft.at(n))
                step(dve.tensor_scalar(v, dtT[:, :], dt_bias, None, ALU.add))
                step(dve.tensor_scalar(mx, v, 0.0, None, ALU.max))
                step(dve.scalar_tensor_tensor(out=av, in0=mx, scalar=2.0, in1=v, op0=ALU.mult, op1=ALU.subtract))
                dve.wait_ge(softe.sem, softe.at(1))
                step(dve.tensor_scalar(t_, e, 2.0, None, ALU.add))
                step(dve.reciprocal(s2, t_))
                step(dve.tensor_tensor(s, e, s2, ALU.mult))
                step(dve.tensor_tensor(s2, s, s, ALU.mult))
                step(dve.tensor_scalar(p, s2, 1.0 / 15, None, ALU.mult))
                for k in (13, 11, 9, 7, 5, 3):
                    step(dve.scalar_tensor_tensor(out=p, in0=p, scalar=1.0 / k, in1=s2, op0=ALU.add, op1=ALU.mult))
                step(dve.scalar_tensor_tensor(out=p, in0=p, scalar=1.0, in1=s, op0=ALU.add, op1=ALU.mult))
                step(dve.scalar_tensor_tensor(out=dtT[:, :], in0=p, scalar=2.0, in1=mx, op0=ALU.mult, op1=ALU.add))
                dve.wait_ge(softe.sem, softe.at(2))
                dve.tensor_scalar(adT[:, :], dtT[:, :], ea[:, :], -1.0, ALU.mult, ALU.mult).then_inc(
                    adt_ready.sem, adt_ready.inc())
                dve.wait_ge(small.sem, small.at(1))
                for dst, o in ((dtk, 0), (adk, 96)):
                    dve.tensor_copy(dst[:, 0:2, :], ps[:, 0, o:o + 64]).then_inc(smalls.sem, smalls.inc())
                    dve.tensor_copy(dst[0:NS, 2, :], ps[0:NS, 0, o + 64:o + 96]).then_inc(smalls.sem, smalls.inc())
                dve.wait_ge(small.sem, small.at(2))
                dve.tensor_copy(ack[:, :, :], ps[:, 1, 0:96]).then_inc(smalls.sem, smalls.inc())
                dve.tensor_copy(tot[:, :, :], ps[:, 1, 96:192]).then_inc(smalls.sem, smalls.inc())
                dve.tensor_copy(acT[:, :], ps[0:HEADS, 2, 0:TOK]).then_inc(smalls.sem, smalls.inc())
                dve.wait_ge(smalls.sem, smalls.at(7))
                dve.tensor_tensor(arg[:, 0:3, :], tot[:, :, :], ack[:, :, :], ALU.subtract).then_inc(
                    decays.sem, decays.inc())
                dve.wait_ge(decays.sem, decays.at(1))
                dve.tensor_tensor(arg[:, 3, :], arg[:, 0, :], tot[:, 1, :], ALU.add).then_inc(decays.sem, decays.inc())
                dve.wait_ge(expand.sem, expand.at(2))
                dve.tensor_copy(dsk[:, :], ps[:, 4, 0:CI]).then_inc(expanded.sem, expanded.inc())
                for c in range(CI):
                    dve.wait_ge(x_turned.sem, x_turned.at(c + 1))
                    b = c % 3 + 5
                    dve.tensor_tensor(
                        XD[:, 0:2, c * P:(c + 1) * P].rearrange("p t (h n) -> p t h n", h=2),
                        ps[:, b, 0:2 * P].rearrange("p (t h n) -> p t h n", t=2, h=2),
                        dtk[:, 0:2, 2 * c:2 * c + 2].unsqueeze(3).to_broadcast([P, 2, 2, 64]), ALU.mult).then_inc(
                        x_moved.sem, x_moved.inc())
                    dve.tensor_tensor(
                        XD[0:NS, 2, c * P:(c + 1) * P].rearrange("p (h n) -> p h n", h=2),
                        ps[0:NS, b, 2 * P:3 * P].rearrange("p (h n) -> p h n", h=2),
                        dtk[0:NS, 2, 2 * c:2 * c + 2].unsqueeze(2).to_broadcast([NS, 2, 64]), ALU.mult).then_inc(
                        x_moved.sem, x_moved.inc())
                dve.wait_ge(x_moved.sem, x_moved.at(2 * CI))
                dve.wait_ge(dec_ready.sem, dec_ready.at(1))
                for n_, (t, k) in enumerate(((0, 0), (0, 3), (1, 1))):
                    dve.tensor_tensor(
                        heads_of(U[:, n_, :]), heads_of(XD[:, t, :]),
                        dec[:, k, :].unsqueeze(2).to_broadcast([P, HEADS, 64]), ALU.mult).then_inc(
                        scaled.sem, scaled.inc())
                dve.tensor_tensor(heads_of(U2[:, :]), heads_of(XD[0:NS, 2, :]),
                                  dec[0:NS, 2, :].unsqueeze(2).to_broadcast([NS, HEADS, 64]), ALU.mult).then_inc(
                    scaled.sem, scaled.inc())
                dve.wait_ge(cleared.sem, cleared.at(1))
                for g in range(GROUPS):
                    dve.wait_ge(cb_mm.sem, cb_mm.at(g + 1))
                    dve.tensor_tensor(
                        cbm[:, g, 0:SEQ].rearrange("p (t n) -> p t n", t=2),
                        ps[:, g, 0:SEQ].rearrange("p (t n) -> p t n", t=2),
                        tri.unsqueeze(1).to_broadcast([P, 2, P]), ALU.mult).then_inc(cb_ready.sem, cb_ready.inc())
                    dve.tensor_tensor(cbm[0:NS, g, SEQ:TOK], ps[0:NS, g, SEQ:TOK],
                                      tris[0:NS, 0:NS], ALU.mult).then_inc(cb_ready.sem, cb_ready.inc())

            @block.scalar
            def _(act):
                act.wait_ge(soft.sem, soft.at(3))
                act.activation(e, av, ACT.Exp, scale=-1.0).then_inc(softe.sem, softe.inc())
                act.activation(ea[:, :], a_log, ACT.Exp).then_inc(softe.sem, softe.inc())
                act.wait_ge(decays.sem, decays.at(2))
                act.activation(dec[:, :, :], arg[:, :, :], ACT.Exp).then_inc(dec_ready.sem, dec_ready.inc())
                act.wait_ge(expand.sem, expand.at(1))
                act.activation(EA[:, :, :], ps[:, 3, :], ACT.Exp).then_inc(expanded.sem, expanded.inc())
                for g in range(GROUPS):
                    act.wait_ge(x_turned.sem, x_turned.at(CI + g + 1))
                    b = (CI + g) % 3 + 5
                    act.activation(Bt[:, 0:2, g * P:(g + 1) * P], ps[:, b, 0:2 * P], ACT.Copy).then_inc(
                        b_moved.sem, b_moved.inc())
                    act.activation(Bt[0:NS, 2, g * P:(g + 1) * P], ps[0:NS, b, 2 * P:3 * P], ACT.Copy).then_inc(
                        b_moved.sem, b_moved.inc())
                act.wait_ge(state_mm.sem, state_mm.at(1))
                act.activation(S0[:, :], ps[:, 0:4, :], ACT.Copy).then_inc(states_out.sem, states_out.inc())
                act.wait_ge(state_mm.sem, state_mm.at(2))
                act.activation(Fs[:, :], ps[:, 4:8, :], ACT.Copy).then_inc(states_out.sem, states_out.inc())
                act.wait_ge(state_mm.sem, state_mm.at(3))
                act.activation(tl[:, 0:2048], ps[0:27, 4:8, :], ACT.Copy).then_inc(states_out.sem, states_out.inc())
                act.wait_ge(state_mm.sem, state_mm.at(4))
                act.activation(tl[:, 2048:3072], ps[0:27, 4:6, :], ACT.Copy).then_inc(states_out.sem, states_out.inc())

            @block.tensor
            def _(pe):
                pe.wait_ge(adt_ready.sem, adt_ready.at(1))
                for src, o in ((dtT, 0), (adT, 96)):
                    for t, n in TILES:
                        mm = pe.transpose(ps[0:n, 0, o + 32 * t:o + 32 * t + 32], src[:, cols_of(t)],
                                          ident[0:HEADS, 0:HEADS])
                mm.then_inc(small.sem, small.inc())
                pe.wait_ge(smalls.sem, smalls.at(4))
                for t, n in TILES:
                    until, all_ = (tri, ones) if t < 2 else (tris, same)
                    pe.matmul(ps[:, 1, 32 * t:32 * t + 32], until[0:n, :], adk[0:n, t, :], start=True, stop=True)
                    pe.matmul(ps[:, 1, 96 + 32 * t:128 + 32 * t], all_[0:n, :], adk[0:n, t, :], start=True, stop=True)
                    mm = pe.matmul(ps[0:HEADS, 2, cols_of(t)], adk[0:n, t, :], until[0:n, 0:n], start=True, stop=True)
                mm.then_inc(small.sem, small.inc())
                pe.wait_ge(smalls.sem, smalls.at(7))
                for bank, row, n in ((3, acT[:, SEQ:TOK], NS), (4, perhead[:, 2, i_ssd:i_ssd + 1], 1)):
                    for h in range(HEADS):
                        one = ident[0:HEADS, h:h + 1].to_broadcast([HEADS, 64])
                        o, c = h % 2 * 64, h // 2
                        mm = pe.matmul(ps[o:o + 64, bank, c * n:(c + 1) * n], one, row, start=True, stop=True)
                    mm.then_inc(expand.sem, expand.inc())
                for c in range(CI + GROUPS):
                    if c >= 3:
                        pe.wait_ge(x_moved.sem, x_moved.at(min(2 * (c - 3 + 1), 2 * CI)))
                        if c - 3 >= CI:
                            pe.wait_ge(b_moved.sem, b_moved.at(2 * (c - 3 - CI + 1)))
                    for t, n in TILES:
                        mm = pe.transpose(ps[0:n, c % 3 + 5, t * P:(t + 1) * P], XB[:, c, cols_of(t)], ident)
                    mm.then_inc(x_turned.sem, x_turned.inc())
                pe.wait_ge(scaled.sem, scaled.at(1))
                pe.wait_ge(b_moved.sem, b_moved.at(2 * GROUPS))
                pe.wait_ge(expanded.sem, expanded.at(2))
                for g in range(GROUPS):
                    mm = pe.matmul(ps[:, g, :], Bt[:, 0, g * P:(g + 1) * P], U[:, 0, g * 512:(g + 1) * 512],
                                   start=True, stop=True)
                mm.then_inc(state_mm.sem, state_mm.inc())
                pe.wait_ge(scaled.sem, scaled.at(3))
                for c in range(CI):
                    o = ps[:, 4 + c // 4, (c % 4) * P:(c % 4 + 1) * P]
                    g = c // 4
                    for t in range(2):
                        mm = pe.matmul(o, U[:, 1 + t, c * P:(c + 1) * P], Bt[:, t, g * P:(g + 1) * P],
                                       start=(t == 0), stop=(t == 1))
                mm.then_inc(state_mm.sem, state_mm.inc())
                pe.wait_ge(states_out.sem, states_out.at(1))
                for g in range(GROUPS):
                    for t, n in TILES:
                        mm = pe.matmul(ps[0:n, g, cols_of(t)], XB[:, CI + g, cols_of(t)],
                                       XB[:, CI + GROUPS + g, cols_of(t)], start=True, stop=True)
                    mm.then_inc(cb_mm.sem, cb_mm.inc())
                pe.wait_ge(states_out.sem, states_out.at(2))
                for c in range(CX):
                    if c == 16:
                        mm.then_inc(state_mm.sem, state_mm.inc())
                        pe.wait_ge(states_out.sem, states_out.at(3))
                    mm = pe.transpose(ps[0:27, 4 + c // 4 % 4, (c % 4) * P:(c % 4 + 1) * P],
                                      tail[:, c, :, :], ident)
                mm.then_inc(state_mm.sem, state_mm.inc())

            @block.sync
            def _(sp):
                sp.wait_ge(states_out.sem, states_out.at(2))
                sp.dma_start(
                    O["ssm_prompt"][i_ssd, 0].rearrange("(c h) p n -> (h p) c n", h=2),
                    Fs.rearrange("p (c n) -> p c n", c=CI)).then_inc(stored.sem, stored.inc())
                sp.wait_ge(states_out.sem, states_out.at(4))
                sp.dma_start(O["ssm_conv_prompt"][i_ssd, 0], tl[0:3, :]).then_inc(stored.sem, stored.inc())
                sp.dma_start(O["ssm_conv_sample"][i_ssd].rearrange("b w n -> (b w) n"), tl[3:27, :]).then_inc(
                    stored.sem, stored.inc())
                sp.wait_ge(stored.sem, stored.at(3))

        h_in = [S(f"state_loaded{r}", 16) for r in range(2)]
        h_out = [S(f"state_stored{r}", 16) for r in range(2)]
        h_turned, h_moved, b_masked, y_state, c_staged, outer, updated, y_rows, y_turned = (
            S(n) for n in ("state_turned", "state_moved", "b_masked", "y_state", "c_staged",
                           "state_outer", "state_updated", "y_rows_moved", "y_rows_turned"))
        with phase() as (block, sb):
            H, HT = sb("H", [P, 2, CI, P]), sb("HT", [P, 2, CI, P])
            Bm = sb("Bm", [NS, 2, GROUPS * N_STATE])
            Cm, none = sb("Cm", [P, 2, GROUPS, NS]), sb("none", [P, GROUPS, NS])
            yrow = sb("yrow", [NS, D_INNER])
            src, dst = A["state_ssm"][i_ssd], O["ssm_sample"][i_ssd]
            rows_of = lambda ap: ap.rearrange("b h p n -> (b h p) n")
            of_b = lambda ap, b: rows_of(ap)[ds(b * D_INNER, D_INNER), :].rearrange(
                "(c p) n -> p c n", p=P)

            def store(sp, b):
                sp.wait_ge(updated.sem, updated.at(CI * (b + 1)))
                sp.dma_start(of_b(dst, b), H[:, b % 2, :, :]).then_inc(h_out[b % 2].sem, h_out[b % 2].inc())

            @block.sync
            def _(sp):
                for b in range(NB):
                    if b >= 2:
                        sp.wait_ge(h_out[b % 2].sem, h_out[b % 2].at(b // 2))
                    sp.dma_start(H[:, b % 2, :, :], of_b(src, b)).then_inc(h_in[b % 2].sem, h_in[b % 2].inc())
                    if b >= 1:
                        store(sp, b - 1)
                store(sp, NB - 1)
                for r in range(2):
                    sp.wait_ge(h_out[r].sem, h_out[r].at(NB // 2))

            @block.tensor
            def _(pe):
                def body(b, r, half):
                    pe.wait_ge(h_in[r].sem, h_in[r].at(half + 1))
                    for q in range(4):
                        pe.wait_ge(h_moved.sem, h_moved.at(4 * b + q - 1))
                        for k in range(4):
                            mm = pe.transpose(ps[:, q % 2, k * P:(k + 1) * P], H[:, r, 4 * q + k, :], ident)
                        mm.then_inc(h_turned.sem, h_turned.inc())
                    pe.wait_ge(b_masked.sem, b_masked.at(b + 1))
                    for q in range(4):
                        pe.wait_ge(updated.sem, updated.at(16 * b + 4 * q - 4))
                        for k in range(4):
                            c = 4 * q + k
                            mm = pe.matmul(ps[:, 2 + q % 2, k * P:(k + 1) * P], U2[:, c * P:(c + 1) * P],
                                           Bm[:, r, q * P:(q + 1) * P], start=True, stop=True)
                        mm.then_inc(outer.sem, outer.inc())
                    pe.wait_ge(h_moved.sem, h_moved.at(4 * b + 4))
                    pe.wait_ge(c_staged.sem, c_staged.at(2 * b + 3))
                    for g in range(GROUPS):
                        mm = pe.matmul(ps[0:NS, 4 + g, :], Cm[:, r, g, :], HT[:, r, 4 * g:4 * g + 4, :],
                                       start=False, stop=True, skip_group_check=True)
                    mm.then_inc(y_state.sem, y_state.inc())
                pe.wait_ge(c_staged.sem, c_staged.at(1))
                for g in range(GROUPS):
                    pe.matmul(ps[0:NS, 4 + g, :], none[:, 0, :], XD[:, 0, 0:512], start=True, stop=True)
                with repeat(pe, NB // 2) as it:
                    for r in range(2):
                        body(it * 2 + r, r, it)
                pe.wait_ge(y_rows.sem, y_rows.at(1))
                pe.wait_ge(h_moved.sem, h_moved.at(4 * NB))
                for c in range(CI):
                    mm = pe.transpose(ps[:, 0, c * NS:(c + 1) * NS], yrow[:, c * P:(c + 1) * P], ident[0:NS, 0:NS])
                mm.then_inc(y_turned.sem, y_turned.inc())

            @block.gpsimd
            def _(pool):
                pool.memset(none[:, :, :], 0.0).then_inc(c_staged.sem, c_staged.inc())
                pool.wait_ge(c_staged.sem, c_staged.at(1))
                for b in range(NB):
                    r, cols = b % 2, slice(SEQ + b * T, SEQ + (b + 1) * T)
                    pool.wait_ge(y_state.sem, y_state.at(b - 1))
                    pool.tensor_copy(Cm[:, r, :, :], none[:, :, :]).then_inc(c_staged.sem, c_staged.inc())
                    pool.wait_ge(c_staged.sem, c_staged.at(2 * b + 2))
                    pool.tensor_copy(Cm[:, r, :, b * T:(b + 1) * T], XB[:, CI + GROUPS:CX, cols]).then_inc(
                        c_staged.sem, c_staged.inc())

            @block.scalar
            def _(act):
                with repeat(act, NB // 2) as it:
                    for r in range(2):
                        b = it * 2 + r
                        act.wait_ge(y_state.sem, y_state.at(b - 1))
                        for q in range(4):
                            act.wait_ge(h_turned.sem, h_turned.at(4 * b + q + 1))
                            act.activation(HT[:, r, 4 * q:4 * q + 4, :], ps[:, q % 2, :], ACT.Copy).then_inc(
                                h_moved.sem, h_moved.inc())

            @block.vector
            def _(dve):
                with repeat(dve, NB // 2) as it:
                    for r in range(2):
                        b = it * 2 + r
                        dve.wait_ge(outer.sem, outer.at(4 * b - 4))
                        dve.tensor_scalar(Bm[:, r, :], Bt[0:NS, 2, :],
                                          cst[0:NS, ds(b + C_BCOL, 1)], None, ALU.mult).then_inc(
                            b_masked.sem, b_masked.inc())
                        for c in range(CI):
                            if c % 4 == 0:
                                dve.wait_ge(outer.sem, outer.at(4 * b + c // 4 + 1))
                            if c == 0:
                                dve.wait_ge(h_turned.sem, h_turned.at(4 * b + 4))
                            dve.scalar_tensor_tensor(
                                out=H[:, r, c, :], in0=H[:, r, c, :], scalar=EA[:, c, ds(b * T + (T - 1), 1)],
                                in1=ps[:, 2 + c // 4 % 2, (c % 4) * P:(c % 4 + 1) * P],
                                op0=ALU.mult, op1=ALU.add).then_inc(updated.sem, updated.inc())
                dve.wait_ge(y_state.sem, y_state.at(NB))
                dve.tensor_copy(yrow.rearrange("p (g n) -> p g n", g=GROUPS), ps[0:NS, 4:8, :]).then_inc(
                    y_rows.sem, y_rows.inc())
                dve.wait_ge(y_turned.sem, y_turned.at(1))
                dve.tensor_copy(yS[:, :, :], ps[:, 0, :].rearrange("p (c n) -> p c n", n=NS)).then_inc(
                    y_rows.sem, y_rows.inc())

        spread, sub_ready, exp_ready, w_ready, y_done, y_taken, gated, y_sq, y_sum, y_mean, y_rstd = (
            S(n) for n in ("ac_spread", "decay_diff", "decay_exp", "w_ready", "y_products", "y_taken",
                           "y_gated", "y_squares", "y_sumsq", "y_mean", "y_rstd"))
        with phase() as (block, sb):
            DEEP = 4
            spread_bank = (0, 1, 6, 7)
            M, E = sb("M", [P, DEEP, TOK]), sb("E", [P, DEEP, TOK + P])
            W = sb("W", [P, DEEP, TOK + P])
            yt, sqy, rs = sb("yt", [P, 2, TOK]), sb("sqy", [P, 2, TOK]), sb("rsy", [P, 3, GROUPS, TOK])

            def sum_sq(pe, c):
                pe.wait_ge(y_sq.sem, y_sq.at(c + 1))
                if c >= 8 and c % 4 == 0:
                    pe.wait_ge(y_mean.sem, y_mean.at(c // 4 - 1))
                pe.matmul(ps[:, 4 + c // 4 % 2, 0:TOK], ones, sqy[:, c % 2, :],
                          start=(c % 4 == 0), stop=(c % 4 == 3)).then_inc(y_sum.sem, y_sum.inc())

            def take(dve, c):
                r = c % 2
                dve.wait_ge(y_done.sem, y_done.at(2 * c + 2))
                if c >= 2:
                    dve.wait_ge(gated.sem, gated.at(c - 2 + 1))
                dve.scalar_tensor_tensor(out=yt[:, r, :], in0=XB[:, c, :], scalar=dsk[:, c:c + 1],
                                         in1=ps[:, 2 + r, 0:TOK], op0=ALU.mult, op1=ALU.add).then_inc(
                    y_taken.sem, y_taken.inc())
                dve.wait_ge(smalls.sem, smalls.at(1 + c))
                dve.wait_ge(y_taken.sem, y_taken.at(c + 1))
                dve.tensor_tensor(yt[:, r, SEQ:TOK], yt[:, r, SEQ:TOK], yS[:, c, :], ALU.add).then_inc(
                    smalls.sem, smalls.inc())
                dve.wait_ge(smalls.sem, smalls.at(2 + c))
                dve.tensor_tensor(Z[:, c, :], Z[:, c, :], yt[:, r, :], ALU.mult).then_inc(gated.sem, gated.inc())

            def mean(dve, g):
                dve.wait_ge(y_sum.sem, y_sum.at(4 * g + 4))
                dve.tensor_scalar(rs[:, 0, g, :], ps[:, 4 + g % 2, 0:TOK], 1.0 / 512, EPS, ALU.mult, ALU.add).then_inc(
                    y_mean.sem, y_mean.inc())

            def square(act, c):
                act.wait_ge(gated.sem, gated.at(c + 1))
                if c >= 2:
                    act.wait_ge(y_sum.sem, y_sum.at(c - 2 + 1))
                act.activation(sqy[:, c % 2, :], Z[:, c, :], ACT.Square).then_inc(y_sq.sem, y_sq.inc())

            @block.tensor
            def _(pe):
                def spread_head(h):
                    if h >= DEEP:
                        pe.wait_ge(exp_ready.sem, exp_ready.at(2 * (h - DEEP + 1)))
                    pe_ = ident[0:HEADS, h:h + 1].to_broadcast([HEADS, P])
                    pe.matmul(ps[:, spread_bank[h % DEEP], 0:TOK], pe_, acT[:, :], start=True, stop=True).then_inc(
                        spread.sem, spread.inc())
                for h in range(DEEP):
                    spread_head(h)
                for h in range(HEADS):
                    c, o, bank = h // 2, (h % 2) * 64, 2 + h // 2 % 2
                    if h % 2 == 0 and c >= 2:
                        pe.wait_ge(y_taken.sem, y_taken.at(c - 2 + 1))
                    pe.wait_ge(w_ready.sem, w_ready.at(2 * (h + 1)))
                    hs = slice(h * 64, h * 64 + 64)
                    r = h % DEEP
                    y = ps[o:o + 64, bank, :]
                    pe.matmul(y[:, 0:P], XD[:, 0, hs], W[:, r, 0:P], start=True, stop=True)
                    pe.matmul(y[:, P:2 * P], XD[:, 1, hs], W[:, r, P:2 * P], start=True, stop=False)
                    pe.matmul(y[:, P:2 * P], S0[:, hs], W[:, r, TOK:TOK + P], start=False, stop=True)
                    pe.matmul(y[:, 2 * P:TOK], XD[0:NS, 2, hs], W[0:NS, r, 2 * P:TOK],
                              start=True, stop=True).then_inc(y_done.sem, y_done.inc())
                    if h + DEEP < HEADS:
                        spread_head(h + DEEP)
                    if h % 2 == 1 and c >= 1:
                        sum_sq(pe, c - 1)
                sum_sq(pe, CI - 1)

            @block.vector
            def _(dve):
                dve.tensor_tensor(yS[:, :, :], yS[:, :, :], EA[:, :, :], ALU.mult).then_inc(smalls.sem, smalls.inc())
                for h in range(HEADS):
                    r = h % DEEP
                    dve.wait_ge(spread.sem, spread.at(h + 1))
                    if h >= DEEP:
                        dve.wait_ge(exp_ready.sem, exp_ready.at(2 * (h - DEEP) + 1))
                    for t in range(3):
                        dve.tensor_scalar(M[:, r, cols_of(t)], ps[:, spread_bank[r], cols_of(t)],
                                          ack[:, t, h:h + 1], 0.0, ALU.subtract, ALU.min).then_inc(
                            sub_ready.sem, sub_ready.inc())
                    if h >= 3 and h % 2 == 1:
                        take(dve, h // 2 - 1)
                        if h // 2 - 1 in (6, 10, 14):
                            mean(dve, (h // 2 - 1) // 4 - 1)
                take(dve, CI - 1)
                mean(dve, GROUPS - 1)
                dve.wait_ge(y_rstd.sem, y_rstd.at(2))
                for c in range(CI):
                    g = V_SSM + i_ssd * CI + c
                    dve.scalar_tensor_tensor(out=Z[:, c, :], in0=Z[:, c, :], scalar=vec[:, 0, g:g + 1],
                                             in1=rs[:, 2, c // 4, :], op0=ALU.mult, op1=ALU.mult).then_inc(
                        gated.sem, gated.inc())

            @block.scalar
            def _(act):
                for h in range(HEADS):
                    r = h % DEEP
                    act.wait_ge(sub_ready.sem, sub_ready.at(3 * (h + 1)))
                    if h >= DEEP:
                        act.wait_ge(w_ready.sem, w_ready.at(2 * (h - DEEP) + 2))
                    act.activation(E[:, r, 0:TOK], M[:, r, :], ACT.Exp).then_inc(exp_ready.sem, exp_ready.inc())
                    act.activation(E[:, r, TOK:TOK + P], ps[:, spread_bank[r], P:2 * P], ACT.Exp).then_inc(
                        exp_ready.sem, exp_ready.inc())
                    if h >= 5 and h % 2 == 1:
                        square(act, h // 2 - 2)
                for c in (CI - 2, CI - 1):
                    square(act, c)
                act.wait_ge(y_mean.sem, y_mean.at(GROUPS))
                act.activation(rs[:, 1, :, :], rs[:, 0, :, :], ACT.Ln).then_inc(y_rstd.sem, y_rstd.inc())
                act.wait_ge(y_rstd.sem, y_rstd.at(1))
                act.activation(rs[:, 2, :, :], rs[:, 1, :, :], ACT.Exp, scale=-0.5).then_inc(y_rstd.sem, y_rstd.inc())

            @block.gpsimd
            def _(pool):
                for h in range(HEADS):
                    r, g = h % DEEP, h // 8
                    if h >= DEEP:
                        pool.wait_ge(y_done.sem, y_done.at(h - DEEP + 1))
                    pool.wait_ge(exp_ready.sem, exp_ready.at(2 * h + 1))
                    pool.tensor_tensor(W[:, r, 0:TOK], E[:, r, 0:TOK], cbm[:, g, :], ALU.mult).then_inc(
                        w_ready.sem, w_ready.inc())
                    pool.wait_ge(exp_ready.sem, exp_ready.at(2 * h + 2))
                    pool.tensor_tensor(W[:, r, TOK:TOK + P], E[:, r, TOK:TOK + P],
                                       XB[:, CI + GROUPS + g, P:2 * P], ALU.mult).then_inc(w_ready.sem, w_ready.inc())

        linear_phase([(Linear(KD, CI, 1, columns(A["ssm_w_out"][i_ssd], CI, 1)),
                       lambda sb, parts: residual(sb, parts, CI))], nxt, source=lambda c: Z[:, c, :])
        mem.close()

    stored = S("stored", 16)
    flat = ps.rearrange("p b n -> p (b n)")
    kv_rows = lambda ap, b: ap[0, b].rearrange("w k h d -> w (k h d)")
    qkv_moved = S("qkv_moved")

    def qkv_evac(dst):
        def evac(sb, parts):
            def act_before(act, i, r, g):
                act.wait_ge(blocks_done.sem, g + 1)
                act.activation(dst[:, ds(2 * i, 2), :], ps[:, 2 * r:2 * r + 2, 0:TOK], ACT.Copy).then_inc(
                    out_read.sem, out_read.inc())
            return dict(plan=two_banks(parts, range(KD)), act=(act_before, None))
        return evac

    def residual2(sb, parts, kk):
        def dve_before(dve, i, r, g):
            dve.wait_ge(blocks_done.sem, g + 1)
            xc = x[:, ds(2 * i, 2), :]
            dve.tensor_tensor(xc, xc, ps[:, 2 * r:2 * r + 2, 0:TOK], ALU.add).then_inc(out_read.sem, out_read.inc())
        return dict(plan=two_banks(parts, range(kk)), dve=(dve_before, None))

    hsq, hsum, hmean, hrstd, hnormed = (S(n) for n in ("head_squares", "head_sumsq", "head_mean", "head_rstd",
                                                      "heads_normed"))
    hankel_in, bias_turned, bias_moved, gains = (S(n, s) for n, s in (("hankel_loaded", 16), ("bias_turned", 1), ("bias_moved", 1), ("gains", 1)))

    def norm_heads(block, sb, X, nq, nk, vq, within=blk64, width=HD, scale=HD ** -0.5):
        n = nq + nk
        sq, rs = sb("hsq", [P, n, TOK]), sb("hrs", [P, n, TOK])
        gq = sb("gq", [P, 1])
        groups = [(a, min(a + 4, n)) for a in range(0, n, 4)]

        def act_part(act):
            for a, b in groups:
                act.activation(sq[:, a:b, :], X[:, a:b, :], ACT.Square).then_inc(hsq.sem, hsq.inc())
            for k, (a, b) in enumerate(groups):
                act.wait_ge(hmean.sem, hmean.at(k + 1))
                act.activation(sq[:, a:b, :], rs[:, a:b, :], ACT.Ln).then_inc(hrstd.sem, hrstd.inc())
                act.wait_ge(hrstd.sem, hrstd.at(2 * k + 1))
                act.activation(rs[:, a:b, :], sq[:, a:b, :], ACT.Exp, scale=-0.5).then_inc(hrstd.sem, hrstd.inc())

        def pe_part(pe):
            for k, (a, b) in enumerate(groups):
                pe.wait_ge(hsq.sem, hsq.at(k + 1))
                if k >= 2:
                    pe.wait_ge(hmean.sem, hmean.at(k - 1))
                for c in range(a, b):
                    mm = pe.matmul(ps[:, c % 8, 0:TOK], within, sq[:, c, :], start=True, stop=True)
                mm.then_inc(hsum.sem, hsum.inc())

        def dve_part(dve):
            dve.tensor_scalar(gq[:, :], vec[:, 0, vq:vq + 1], scale, None, ALU.mult).then_inc(gains.sem, gains.inc())
            for k, (a, b) in enumerate(groups):
                dve.wait_ge(hsum.sem, hsum.at(k + 1))
                dve.tensor_scalar(rs[:, a:b, :], ps[:, a % 8:a % 8 + b - a, 0:TOK], 1.0 / width, EPS,
                                  ALU.mult, ALU.add).then_inc(hmean.sem, hmean.inc())
            dve.wait_ge(gains.sem, gains.at(1))
            for k, (a, b) in enumerate(groups):
                dve.wait_ge(hrstd.sem, hrstd.at(2 * k + 2))
                for lo, hi, gain in ((a, min(b, nq), gq[:, :]), (max(a, nq), b, vec[:, 0, vq + 1:vq + 2])):
                    if lo < hi:
                        ins = dve.scalar_tensor_tensor(out=X[:, lo:hi, :], in0=X[:, lo:hi, :], scalar=gain,
                                                       in1=rs[:, lo:hi, :], op0=ALU.mult, op1=ALU.mult)
                ins.then_inc(hnormed.sem, hnormed.inc())
        return act_part, pe_part, dve_part, len(groups)

    def prompt_bias(sb, kinds):
        BT = sb("BT", [P, NH, 2, P])
        HK = sb("HK", [P, NH, 2, P])

        def sp_part(sp):
            for kind, h0, h1 in kinds:
                for tile, off in ((0, P), (1, 0)):
                    src = bass.AP(dist_tab.tensor, (kind * NH + h0) * 512 + off, [[1, P], [512, h1 - h0], [1, P]])
                    sp.dma_start(HK[:, h0:h1, tile, :], src).then_inc(hankel_in.sem, hankel_in.inc())

        def pe_part(pe, base=0):
            pe.wait_ge(hankel_in.sem, hankel_in.at(2 * len(kinds)))
            for q in range(6):
                if q >= 2:
                    pe.wait_ge(bias_moved.sem, bias_moved.at(q - 1))
                for k in range(4):
                    h, tile = (4 * q + k) // 2, (4 * q + k) % 2
                    mm = pe.matmul(ps[:, 6 + q % 2, k * P:(k + 1) * P], HK[:, h, tile, :], cst[:, C_ANTI:C_ANTI + P],
                                   start=True, stop=True)
                mm.then_inc(bias_turned.sem, bias_turned.inc())

        def act_part(act):
            for q in range(6):
                act.wait_ge(bias_turned.sem, bias_turned.at(q + 1))
                act.activation(BT.rearrange("p h t k -> p (h t k)")[:, q * 512:(q + 1) * 512],
                               ps[:, 6 + q % 2, :], ACT.Copy).then_inc(bias_moved.sem, bias_moved.inc())
        return BT, sp_part, pe_part, act_part

    KEYS = ((1, 0, 512), (0, 512, 128), (2, 640, 256))
    N_OLD, N_ALL = 896, 992

    def swa_first(layer):
        return Linear(9, KD, 2, columns(A["swa_w_qkv"][0], KD, 2))

    kv_turned, kv_moved, sc_done, sc_ready, mx_ready, p_ready, diag_ready, pt_done, pt_moved, pv_done, o_moved = (
        S(n) for n in ("kv_turned", "kv_moved", "scores", "scores_biased", "row_max", "probs", "row_scale",
                       "probs_turned", "probs_moved", "pv", "out_moved"))
    k_turned, k_moved_a, k_moved_v, q_staged, old_scored = (
        S(n) for n in ("keys_turned", "keys_moved_act", "keys_moved_dve", "queries_staged", "old_scored"))
    kv_in = [S(f"cache_keys_loaded{r}", 16) for r in range(2)]
    out_staged, out_turned = S("out_staged"), S("out_turned")
    v_in = [S(f"cache_values_loaded{r}", 16) for r in range(2)]

    def swa(layer, nxt):
        mem = ExitStack()

        def keep(name, shape, dt=F32):
            return mem.enter_context(nc.sbuf_tensor(f"{name}_L{layer}", shape, dt))
        X = keep("QKV", [P, 18, TOK])
        linear_phase([(swa_first(layer), qkv_evac(X))], Linear(4, 6, 2, columns(A["swa_w_out"][0], 6, 2)),
                     norm=V_MIX + layer * KD)
        OT = keep("OT", [P, 6, TOK])
        KV = keep("KV", [P, 3, 2, NH * HD])

        with phase() as (block, sb):
            act_norm, pe_norm, dve_norm, n_norm = norm_heads(block, sb, X, 6, 6, V_QK)
            BT, sp_bias, pe_bias, act_bias = prompt_bias(sb, [(g, 4 * g, 4 * g + 4) for g in range(3)])
            Sb, PT = sb("Sb", [P, 2, 3, 2 * P]), sb("PT", [P, 2, 6, P])
            st, DR = sb("st", [P, 2, 3]), sb("DR", [P, 2, P])
            units = [(qt, hh) for qt in range(2) for hh in range(GH)]
            flat = ps.rearrange("p b n -> p (b n)")
            nk_of = lambda qt: P * (qt + 1)

            @block.sync
            def _(sp):
                sp_bias(sp)
                sp.wait_ge(kv_moved.sem, kv_moved.at(24))
                n = 0
                for g in range(3):
                    cols = slice(g * GH * HD, (g + 1) * GH * HD)
                    out = O[f"swa_kv{g}_prompt"][0, 0].rearrange("w k h d -> w k (h d)")
                    for t in ((1,) if g == 0 else (0, 1)):
                        rows = slice(0, P) if g == 0 else slice(t * P, (t + 1) * P)
                        sp.dma_start(out[rows], KV[:, t, :, cols]).then_inc(stored.sem, stored.inc())
                        n += 1
                    for b in range(NB):
                        out = O[f"swa_kv{g}_sample"][0, b].rearrange("w k h d -> w k (h d)")
                        keep_ = out.shape[0]
                        sp.dma_start(out[keep_ - T:keep_], KV[b * T:(b + 1) * T, 2, :, cols]).then_inc(
                            stored.sem, stored.inc())
                        n += 1
                sp.wait_ge(stored.sem, stored.at(n))

            def unit(u):
                qt, hh = units[u]
                rows = slice(hh % 2 * 64, hh % 2 * 64 + 64)
                return qt, hh, rows, u % 2

            @block.tensor
            def _(pe):
                pe_norm(pe)
                pe.wait_ge(hnormed.sem, hnormed.at(n_norm))
                for c in range(12):
                    if c >= 4:
                        pe.wait_ge(kv_moved.sem, kv_moved.at(2 * (c - 3)))
                    for t, n in TILES:
                        mm = pe.transpose(ps[0:n, c % 4, t * P:(t + 1) * P], X[:, 6 + c, cols_of(t)], ident)
                    mm.then_inc(kv_turned.sem, kv_turned.inc())
                pe_bias(pe)
                pe.wait_ge(kv_moved.sem, kv_moved.at(24))

                def scores(u):
                    qt, hh, rows, r = unit(u)
                    if u >= 2:
                        pe.wait_ge(sc_ready.sem, sc_ready.at(u - 1))
                    for g in range(3):
                        c = 2 * g + hh // 2
                        mm = pe.matmul(flat[:, r * 1024 + g * 256:r * 1024 + g * 256 + nk_of(qt)],
                                       X[rows, c, qt * P:(qt + 1) * P], X[rows, 6 + c, 0:nk_of(qt)],
                                       start=True, stop=True)
                    mm.then_inc(sc_done.sem, sc_done.inc())
                scores(0)
                pe.wait_ge(bias_moved.sem, bias_moved.at(6))
                for u in range(len(units)):
                    if u + 1 < len(units):
                        scores(u + 1)
                    qt, hh, rows, r = unit(u)
                    pe.wait_ge(diag_ready.sem, diag_ready.at(2 * u + 2))
                    pe.wait_ge(p_ready.sem, p_ready.at(u + 1))
                    if u >= 1:
                        pe.wait_ge(pt_moved.sem, pt_moved.at(u))
                    for g in range(3):
                        for kt in range(qt + 1):
                            o = 2048 + (2 * g + kt) * P
                            mm = pe.matmul(flat[:, o:o + P], Sb[:, r, g, kt * P:(kt + 1) * P], DR[:, r, :],
                                           start=True, stop=True)
                    mm.then_inc(pt_done.sem, pt_done.inc())
                    pe.wait_ge(pt_moved.sem, pt_moved.at(u + 1))
                    if u >= 2:
                        pe.wait_ge(o_moved.sem, o_moved.at(u - 1))
                    for g in range(3):
                        h = 4 * g + hh
                        for kt in range(qt + 1):
                            mm = pe.matmul(ps[rows, 6 + r, g * P:(g + 1) * P], KV[:, kt, 1, h * HD:(h + 1) * HD],
                                           PT[:, r, 2 * g + kt, :], start=(kt == 0), stop=(kt == qt))
                    mm.then_inc(pv_done.sem, pv_done.inc())

            @block.scalar
            def _(act):
                act_norm(act)
                act_bias(act)
                for u in range(len(units)):
                    qt, hh, rows, r = unit(u)
                    act.wait_ge(mx_ready.sem, mx_ready.at(u + 1))
                    act.activation(Sb[:, r, :, 0:nk_of(qt)], Sb[:, r, :, 0:nk_of(qt)], ACT.Exp,
                                   bias=st[:, r, 0:1], accum_out=st[:, r, 1:2]).then_inc(p_ready.sem, p_ready.inc())
                    act.wait_ge(pt_done.sem, pt_done.at(u + 1))
                    src = flat[:, 2048:2048 + 768].rearrange("p (g k n) -> p g k n", g=3, k=2)
                    dst = PT[:, r, :, :].rearrange("p (g k) n -> p g k n", k=2)
                    if u >= 2:
                        act.wait_ge(pv_done.sem, pv_done.at(u - 1))
                    act.activation(dst[:, :, 0:qt + 1, :], src[:, :, 0:qt + 1, :], ACT.Copy).then_inc(
                        pt_moved.sem, pt_moved.inc())

            @block.vector
            def _(dve):
                dve_norm(dve)
                for c in range(12):
                    dve.wait_ge(kv_turned.sem, kv_turned.at(c + 1))
                    k, f = c // 6, slice(c % 6 * P, (c % 6 + 1) * P)
                    dve.tensor_copy(KV[:, 0:2, k, f],
                                    ps[:, c % 4, 0:2 * P].rearrange("p (t n) -> p t n", t=2)).then_inc(
                        kv_moved.sem, kv_moved.inc())
                    dve.tensor_copy(KV[0:NS, 2, k, f], ps[0:NS, c % 4, 2 * P:3 * P]).then_inc(
                        kv_moved.sem, kv_moved.inc())
                dve.wait_ge(bias_moved.sem, bias_moved.at(6))

                def front(u):
                    qt, hh, rows, r = unit(u)
                    dve.wait_ge(sc_done.sem, sc_done.at(u + 1))
                    if u >= 2:
                        dve.wait_ge(pt_done.sem, pt_done.at(u - 1))
                    n = nk_of(qt)
                    bias = BT.rearrange("p h t k -> p h (t k)")[:, hh::4, 2 * P - n:2 * P]
                    dve.tensor_tensor(
                        Sb[:, r, :, 0:n], flat[:, r * 1024:r * 1024 + 768].rearrange("p (g n) -> p g n", g=3)[:, :, 0:n],
                        bias, ALU.add).then_inc(sc_ready.sem, sc_ready.inc())
                    dve.wait_ge(sc_ready.sem, sc_ready.at(u + 1))
                    dve.tensor_reduce(st[:, r, 0:1], Sb[:, r, :, 0:n], AX.XY, ALU.max, negate=True).then_inc(
                        mx_ready.sem, mx_ready.inc())
                front(0)
                for u in range(len(units)):
                    if u + 1 < len(units):
                        front(u + 1)
                    qt, hh, rows, r = unit(u)
                    dve.wait_ge(p_ready.sem, p_ready.at(u + 1))
                    dve.reciprocal(st[:, r, 2:3], st[:, r, 1:2]).then_inc(diag_ready.sem, diag_ready.inc())
                    dve.wait_ge(diag_ready.sem, diag_ready.at(2 * u + 1))
                    dve.tensor_scalar(DR[:, r, :], ident, st[:, r, 2:3], None, ALU.mult).then_inc(
                        diag_ready.sem, diag_ready.inc())
                    dve.wait_ge(pv_done.sem, pv_done.at(u + 1))
                    dve.tensor_copy(OT[rows, hh // 2::2, qt * P:(qt + 1) * P],
                                    ps[rows, 6 + r, 0:3 * P].rearrange("p (g n) -> p g n", g=3)).then_inc(
                        o_moved.sem, o_moved.inc())

        with phase() as (block, sb):
            K1, K0 = sb("K1", [P, 2, 4, 512]), sb("K0", [P, 2, 512])
            K2 = sb("K2", [64, 2, 4, 512])
            KT = sb("KT", [P, 2, N_OLD])
            Qall, Qst = sb("Qall", [P, NB, 3, 32]), sb("Qst", [P, 2, 3, 32])
            oh = sb("oh", [33, T, N_OLD + 12])
            rb, LT = sb("rb", [33, NH]), sb("LT", [33, 3, T, 16])
            bias, BN, base = sb("bias", [16, N_OLD]), sb("BN", [16, NB, 3, NS]), sb("base", [16, 12])
            Sb, st, DR, PT = sb("Sb", [16, 2, N_ALL]), sb("st", [16, 2, 3]), sb("DR", [16, 2, 16]), sb("PT", [P, 2, 208])
            OS = sb("OS", [96, 2, 2 * P])
            prep, prep2, prep3 = S("buffers_filled"), S("bias_tables"), S("tables_laid")

            @block.sync
            def _(sp):
                sp.dma_start(oh[:, :, :], A["onehot_swa"]).then_inc(loaded.sem, loaded.inc())
                sp.dma_start(rb[0:32, :], A["rel_bias"]).then_inc(loaded.sem, loaded.inc())
                def load(b, kv, arrived):
                    f, r = slice(kv * 256, kv * 256 + 256), b % 2
                    for dst, src in (
                            (K1[:, r, :, f], kv_rows(A["cache_swa_kv1"], b).rearrange("(t p) n -> p t n", p=P)[:, :, f]),
                            (K0[:, r, f], kv_rows(A["cache_swa_kv0"], b)[:, f]),
                            (K2[:, r, :, f], kv_rows(A["cache_swa_kv2"], b).rearrange(
                                "(a s) n -> a s n", s=16)[:, 0:4, f])):
                        sp.dma_start(dst, src).then_inc(arrived.sem, arrived.inc())
                for b in range(NB):
                    if b >= 2:
                        sp.wait_ge(k_turned.sem, k_turned.at(b - 1))
                    load(b, 0, kv_in[b % 2])
                    if b >= 2:
                        sp.wait_ge(pv_done.sem, pv_done.at(b - 1))
                    load(b, 1, v_in[b % 2])

            @block.gpsimd
            def _(pool):
                pool.memset(Qall[:, :, :, :], 0.0).then_inc(prep.sem, prep.inc())
                pool.memset(PT[:, :, :], 0.0).then_inc(prep.sem, prep.inc())
                pool.memset(LT[:, :, :, :], 0.0).then_inc(prep.sem, prep.inc())
                pool.memset(BN[:, :, :, :], NEG).then_inc(prep.sem, prep.inc())
                pool.wait_ge(prep3.sem, prep3.at(5))
                with repeat(pool, NB // 2) as it:
                    for r in range(2):
                        b = it * 2 + r
                        pool.wait_ge(old_scored.sem, old_scored.at(b - 1))
                        pool.tensor_copy(Qst[:, r:r + 1, :, :], Qall[:, ds(b, 1), :, :]).then_inc(
                            q_staged.sem, q_staged.inc())

            key_tiles = [(1, t, P, t * P) for t in range(4)] + [(0, 0, P, 512)] + \
                [(2, t, 64, 640 + 64 * t) for t in range(4)] + [(3 + g, g, NS, N_OLD + g * NS) for g in (1, 0, 2)]

            def tile_of(kind, t, r, kv, cc):
                f = slice(kv * 256 + cc * P, kv * 256 + (cc + 1) * P)
                return (K0[:, r, f], K1[:, r, t, f], K2[:, r, t, f])[kind]

            @block.tensor
            def _(pe):
                pe.wait_ge(prep3.sem, prep3.at(9))
                for g, lo, n in KEYS:
                    for t in range(T):
                        pe.matmul(ps[0:16, 4 + (lo >= 512), lo % 512:lo % 512 + n], LT[:, g, t, :],
                                  oh[:, t, lo:lo + n], start=(t == 0), stop=(t == 3))
                    for t in range(T):
                        mm = pe.matmul(ps[0:16, 6, g * T:(g + 1) * T], LT[:, g, t, :],
                                       oh[:, t, N_OLD + g * T:N_OLD + (g + 1) * T], start=(t == 0), stop=(t == 3))
                mm.then_inc(prep2.sem, prep2.inc())

                def front(b, r, half, back, before):
                    pe.wait_ge(kv_in[r].sem, kv_in[r].at(3 * (half + 1)))
                    pe.wait_ge(k_moved_a.sem, k_moved_a.at(b))
                    pe.wait_ge(k_moved_v.sem, k_moved_v.at(b))
                    for cc in range(2):
                        for kind, t, n, col in key_tiles[:9]:
                            o = cc * N_OLD + col
                            mm = pe.transpose(flat[:, o:o + n], tile_of(kind, t, r, 0, cc), ident[0:n, 0:n])
                    mm.then_inc(k_turned.sem, k_turned.inc())
                    if before:
                        turn_out(b - 2, r)
                    if back:
                        turn_probs(b - 1, 1 - r)
                    pe.wait_ge(q_staged.sem, q_staged.at(b + 1))
                    pe.wait_ge(sc_ready.sem, sc_ready.at(3 * b))
                    pe.wait_ge(k_moved_a.sem, k_moved_a.at(b + 1))
                    pe.wait_ge(k_moved_v.sem, k_moved_v.at(b + 1))
                    for g, lo, n in KEYS:
                        bank, o = 4 + (lo >= 512), lo % 512
                        for cc in range(2):
                            q = Qst[:, r, g, 16 * cc:16 * cc + 16]
                            pe.matmul(ps[0:16, bank, o:o + n], q, KT[:, cc, lo:lo + n],
                                      start=(cc == 0), stop=(cc == 1))
                        o = 384 + g * NS
                        for cc in range(2):
                            q = Qst[:, r, g, 16 * cc:16 * cc + 16]
                            mm = pe.matmul(ps[0:16, 5, o:o + NS], q, X[:, 6 + 2 * g + cc, SEQ:TOK],
                                           start=(cc == 0), stop=(cc == 1))
                    mm.then_inc(old_scored.sem, old_scored.inc())
                    if back:
                        values(b - 1, 1 - r, half - (1 - r))

                def turn_probs(b, r):
                    pe.wait_ge(diag_ready.sem, diag_ready.at(2 * b + 2))
                    pe.wait_ge(pt_moved.sem, pt_moved.at(3 * b))
                    for n_, (kind, t, n, col) in enumerate(key_tiles):
                        mm = pe.matmul(ps[0:n, 6, 16 * n_:16 * n_ + 16], Sb[:, r, col:col + n], DR[:, r, :],
                                       start=True, stop=True)
                    mm.then_inc(pt_done.sem, pt_done.inc())

                def values(b, r, half):
                    pe.wait_ge(v_in[r].sem, v_in[r].at(3 * (half + 1)))
                    pe.wait_ge(pt_moved.sem, pt_moved.at(3 * b + 3))
                    pe.wait_ge(o_moved.sem, o_moved.at(4 * b))
                    for g in range(3):
                        mine = [(n_, k) for n_, k in enumerate(key_tiles) if k[0] in (g, 3 + g)]
                        for m_, (n_, (kind, t, n, col)) in enumerate(mine):
                            f = slice(256, 512)
                            v = (K0[:, r, f], K1[:, r, t, f], K2[:, r, t, f])[kind] if kind < 3 else \
                                KV[0:NS, 2, 1, g * 256:(g + 1) * 256]
                            mm = pe.matmul(ps[32 * g:32 * g + 32, 7, 0:256], PT[0:n, r, 16 * n_:16 * n_ + 32], v,
                                           start=(m_ == 0), stop=(m_ == len(mine) - 1), tile_position=(0, 32 * g))
                    mm.then_inc(pv_done.sem, pv_done.inc())

                def turn_out(b, r):
                    pe.wait_ge(out_staged.sem, out_staged.at(b + 1))
                    for cc in range(2):
                        mm = pe.transpose(ps[:, 7, 256 + cc * P:256 + cc * P + 96], OS[:, r, cc * P:(cc + 1) * P],
                                          ident[0:96, 0:96])
                    mm.then_inc(out_turned.sem, out_turned.inc())

                pe.wait_ge(prep2.sem, prep2.at(3))
                front(0, 0, 0, False, False)
                front(1, 1, 0, True, False)
                with repeat(pe, NB // 2 - 1) as it:
                    for r in range(2):
                        front(it * 2 + (r + 2), r, it + 1, True, True)
                turn_out(NB - 2, 0)
                turn_probs(NB - 1, 1)
                values(NB - 1, 1, NB // 2 - 1)
                turn_out(NB - 1, 1)

            @block.scalar
            def _(act):
                def front(b, r):
                    act.wait_ge(k_turned.sem, k_turned.at(b + 1))
                    act.wait_ge(old_scored.sem, old_scored.at(b))
                    act.activation(KT.rearrange("p c n -> p (c n)")[:, 0:1024], flat[:, 0:1024], ACT.Copy).then_inc(
                        k_moved_a.sem, k_moved_a.inc())

                def exps(b, r):
                    act.wait_ge(mx_ready.sem, mx_ready.at(b + 1))
                    act.activation(Sb[:, r, :], Sb[:, r, :], ACT.Exp, bias=st[:, r, 0:1],
                                   accum_out=st[:, r, 1:2]).then_inc(p_ready.sem, p_ready.inc())
                front(0, 0)
                with repeat(act, NB // 2 - 1) as it:
                    for r in range(2):
                        exps(it * 2 + r, r)
                        front(it * 2 + (r + 1), 1 - r)
                exps(NB - 2, 0)
                front(NB - 1, 1)
                exps(NB - 1, 1)

            @block.vector
            def _(dve):
                dve.memset(rb[32:33, :], NEG).then_inc(prep3.sem, prep3.inc())
                dve.wait_ge(prep.sem, prep.at(4))
                for half in range(2):
                    for cc in range(2):
                        rows = slice(64 * half, 64 * half + 64)
                        col = 16 * cc + 8 * cc + 4 * half
                        dve.tensor_copy(
                            Qall[rows, :, :, col:col + T].rearrange("p b g t -> p g b t"),
                            X[rows, cc:6:2, SEQ:TOK].rearrange("p g (b t) -> p g b t", b=NB)).then_inc(
                            prep3.sem, prep3.inc())
                dve.wait_ge(loaded.sem, loaded.at(2))
                dve.wait_ge(prep3.sem, prep3.at(1))
                for t in range(T):
                    dve.tensor_copy(LT[:, :, t, t::4], rb.rearrange("p (g h) -> p g h", g=3)).then_inc(
                        prep3.sem, prep3.inc())
                dve.wait_ge(prep2.sem, prep2.at(1))
                dve.tensor_copy(bias[:, :], flat[0:16, 2048:2048 + N_OLD]).then_inc(prep2.sem, prep2.inc())
                dve.tensor_copy(base[:, :], ps[0:16, 6, 0:12]).then_inc(prep2.sem, prep2.inc())
                dve.wait_ge(prep2.sem, prep2.at(3))
                for b in range(NB):
                    dve.tensor_copy(BN[:, b, :, b * T:(b + 1) * T], base.rearrange("p (g t) -> p g t", g=3)).then_inc(
                        prep3.sem, prep3.inc())
                dve.wait_ge(prep3.sem, prep3.at(17))

                def scale(b, r):
                    dve.wait_ge(p_ready.sem, p_ready.at(b + 1))
                    dve.reciprocal(st[:, r, 2:3], st[:, r, 1:2]).then_inc(diag_ready.sem, diag_ready.inc())
                    dve.wait_ge(diag_ready.sem, diag_ready.at(2 * b + 1))
                    dve.tensor_scalar(DR[:, r, :], ident[0:16, 0:16], st[:, r, 2:3], None, ALU.mult).then_inc(
                        diag_ready.sem, diag_ready.inc())

                def probs(b, r):
                    dve.wait_ge(pt_done.sem, pt_done.at(b + 1))
                    dve.wait_ge(pv_done.sem, pv_done.at(b - 1))
                    for n, lo, hi in ((P, 0, 80), (64, 80, 144), (NS, 144, 192)):
                        dve.tensor_copy(PT[0:n, r, lo:hi], ps[0:n, 6, lo:hi]).then_inc(pt_moved.sem, pt_moved.inc())

                def stage_out(b, r):
                    dve.wait_ge(pv_done.sem, pv_done.at(b + 1))
                    dve.tensor_copy(OS[:, r, :], ps[0:96, 7, 0:256]).then_inc(out_staged.sem, out_staged.inc())

                def out(b):
                    dve.wait_ge(out_turned.sem, out_turned.at(b + 1))
                    for cc in range(2):
                        turned_ = ps[:, 7, 256 + cc * P:256 + cc * P + 96].rearrange("p (g n) -> p g n", n=32)
                        for half in range(2):
                            rows, c0 = slice(64 * half, 64 * half + 64), 8 * cc + 4 * half
                            dve.tensor_copy(OT[rows, cc:6:2, ds(b * T + SEQ, T)], turned_[rows, :, c0:c0 + T]).then_inc(
                                o_moved.sem, o_moved.inc())

                def front(b, r, back, before):
                    if back:
                        scale(b - 1, 1 - r)
                    dve.wait_ge(k_turned.sem, k_turned.at(b + 1))
                    dve.wait_ge(old_scored.sem, old_scored.at(b))
                    dve.tensor_copy(KT.rearrange("p c n -> p (c n)")[:, 1024:2 * N_OLD],
                                    flat[:, 1024:2 * N_OLD]).then_inc(k_moved_v.sem, k_moved_v.inc())
                    if before:
                        out(b - 2)
                    if back:
                        probs(b - 1, 1 - r)
                    dve.wait_ge(old_scored.sem, old_scored.at(b + 1))
                    dve.wait_ge(pt_done.sem, pt_done.at(b - 1))
                    dve.tensor_tensor(Sb[:, r, 0:512], ps[0:16, 4, :], bias[:, 0:512], ALU.add).then_inc(
                        sc_ready.sem, sc_ready.inc())
                    dve.tensor_tensor(Sb[:, r, 512:N_OLD], ps[0:16, 5, 0:384], bias[:, 512:N_OLD], ALU.add).then_inc(
                        sc_ready.sem, sc_ready.inc())
                    new = BN.rearrange("p b g t -> p b (g t)")[:, ds(b, 1), :]
                    dve.tensor_tensor(Sb[:, r:r + 1, N_OLD:N_ALL], ps[0:16, 5:6, 384:480], new, ALU.add).then_inc(
                        sc_ready.sem, sc_ready.inc())
                    dve.wait_ge(sc_ready.sem, sc_ready.at(3 * b + 3))
                    dve.tensor_reduce(st[:, r, 0:1], Sb[:, r, :], AX.X, ALU.max, negate=True).then_inc(
                        mx_ready.sem, mx_ready.inc())
                    if back:
                        stage_out(b - 1, 1 - r)
                front(0, 0, False, False)
                front(1, 1, True, False)
                with repeat(dve, NB // 2 - 1) as it:
                    for r in range(2):
                        front(it * 2 + (r + 2), r, True, True)
                out(NB - 2)
                scale(NB - 1, 1)
                probs(NB - 1, 1)
                stage_out(NB - 1, 1)
                out(NB - 1)

        linear_phase([(Linear(4, 6, 2, columns(A["swa_w_out"][0], 6, 2)),
                       lambda sb, parts: residual2(sb, parts, 6))], nxt, source=lambda c: OT[:, c, :])
        mem.close()

    KV_C = 2 * KVH
    QCOLS = 2 * REP * T
    NPAGES = PAST // PAGE

    def kv_out(out):
        return out.rearrange("l b t g m d -> (l b t) (g m d)" if len(out.shape) == 6 else
                             "l b t g n -> (l b t) (g n)")

    def kv_pages(cache):
        return cache[0].rearrange("a p g m d -> a p (g m d)" if len(cache.shape) == 6 else "a p g n -> a p (g n)")

    def diff_first(layer):
        return Linear(10, KD, 2, columns(A["diff_w_qkv"][0], KD, 2))

    pages_in = [S(f"keys_loaded{r}", 16) for r in range(2)]
    values_in = [S(f"values_loaded{r}", 16) for r in range(2)]
    table_in = S("page_table_loaded", 16)
    scaled, out_staged, out_turned = S("probs_scaled"), S("out_staged"), S("out_turned")

    def diff(layer, nxt):
        mem = ExitStack()

        def keep(name, shape, dt=F32):
            return mem.enter_context(nc.sbuf_tensor(f"{name}_L{layer}", shape, dt))
        X = keep("QKV", [P, QD_C + KV_C, TOK])
        out_first = Linear(KD, QD_C, 1, columns(A["diff_w_out"][0], QD_C, 1))
        linear_phase([(diff_first(layer), qkv_evac(X))], out_first, norm=V_MIX + layer * KD)
        OT = keep("OT", [P, QD_C, TOK])
        KV = keep("KV", [P, 3, 2, KVH * P])

        with phase() as (block, sb):
            act_norm, pe_norm, dve_norm, n_norm = norm_heads(block, sb, X, QD_C, KVH, V_QK + 2)
            BT, sp_bias, pe_bias, act_bias = prompt_bias(sb, [(3, 0, NH)])
            Sb, PT = sb("Sb", [P, 2, 2, 2 * P]), sb("PT", [P, 2, 2 * P])
            st = sb("st", [P, 2, 3, 2])
            units = [(qt, h) for qt in range(2) for h in range(NH)]
            nk_of = lambda qt: P * (qt + 1)

            @block.sync
            def _(sp):
                sp_bias(sp)
                sp.wait_ge(kv_moved.sem, kv_moved.at(2 * KV_C))
                for k, name in enumerate(("diff_k", "diff_v")):
                    for t in range(2):
                        out = kv_out(O[name + "_prompt"])
                        sp.dma_start(out[t * P:(t + 1) * P], KV[:, t, k, :]).then_inc(stored.sem, stored.inc())
                    sp.dma_start(kv_out(O[name + "_sample"]), KV[0:NS, 2, k, :]).then_inc(stored.sem, stored.inc())
                sp.wait_ge(stored.sem, stored.at(6))

            def values(pe, u):
                qt, h = units[u]
                r = u % 2
                pe.wait_ge(pt_moved.sem, pt_moved.at(u + 1))
                if u >= 2:
                    pe.wait_ge(o_moved.sem, o_moved.at(u - 1))
                for kt in range(qt + 1):
                    mm = pe.matmul(ps[:, 6 + r, 0:P], KV[:, kt, 1, h // REP * P:(h // REP + 1) * P],
                                   PT[:, r, kt * P:(kt + 1) * P], start=(kt == 0), stop=(kt == qt))
                mm.then_inc(pv_done.sem, pv_done.inc())

            @block.tensor
            def _(pe):
                pe_norm(pe)
                pe.wait_ge(hnormed.sem, hnormed.at(n_norm))
                for c in range(KV_C):
                    if c >= 4:
                        pe.wait_ge(kv_moved.sem, kv_moved.at(2 * (c - 3)))
                    for t, n in TILES:
                        mm = pe.transpose(ps[0:n, c % 4, t * P:(t + 1) * P], X[:, QD_C + c, cols_of(t)], ident)
                    mm.then_inc(kv_turned.sem, kv_turned.inc())
                pe_bias(pe)
                pe.wait_ge(kv_moved.sem, kv_moved.at(2 * KV_C))

                def scores(u):
                    qt, h = units[u]
                    n = nk_of(qt)
                    if u >= 2:
                        pe.wait_ge(sc_ready.sem, sc_ready.at(u - 1))
                    for m in range(2):
                        rows = slice(64 * m, 64 * m + 64)
                        mm = pe.matmul(ps[:, 2 * (u % 2) + m, 0:n], X[rows, h, qt * P:(qt + 1) * P],
                                       X[rows, QD_C + h // REP, 0:n], start=True, stop=True)
                    mm.then_inc(sc_done.sem, sc_done.inc())
                scores(0)
                scores(1)
                pe.wait_ge(bias_moved.sem, bias_moved.at(6))
                for u in range(len(units)):
                    if u + 2 < len(units):
                        scores(u + 2)
                    qt, h = units[u]
                    r = u % 2
                    pe.wait_ge(scaled.sem, scaled.at(2 * u + 2))
                    if u >= 2:
                        pe.wait_ge(pt_moved.sem, pt_moved.at(u - 1))
                    for kt in range(qt + 1):
                        mm = pe.transpose(ps[:, 4 + r, kt * P:(kt + 1) * P], Sb[:, r, 0, kt * P:(kt + 1) * P], ident)
                    mm.then_inc(pt_done.sem, pt_done.inc())
                    if u >= 1:
                        values(pe, u - 1)
                values(pe, len(units) - 1)

            @block.scalar
            def _(act):
                act_norm(act)
                act_bias(act)
                for u in range(len(units) + 1):
                    if u < len(units):
                        qt, h = units[u]
                        r = u % 2
                        act.wait_ge(mx_ready.sem, mx_ready.at(u + 1))
                        for m in range(2):
                            act.activation(Sb[:, r, m, 0:nk_of(qt)], Sb[:, r, m, 0:nk_of(qt)], ACT.Exp,
                                           bias=st[:, r, 0, m:m + 1], accum_out=st[:, r, 1, m:m + 1]).then_inc(
                                p_ready.sem, p_ready.inc())
                    if u >= 1:
                        v, r = u - 1, (u - 1) % 2
                        n = nk_of(units[v][0])
                        act.wait_ge(pt_done.sem, pt_done.at(v + 1))
                        if v >= 2:
                            act.wait_ge(pv_done.sem, pv_done.at(v - 1))
                        act.activation(PT[:, r, 0:n], ps[:, 4 + r, 0:n], ACT.Copy).then_inc(
                            pt_moved.sem, pt_moved.inc())

            @block.vector
            def _(dve):
                dve_norm(dve)
                for c in range(KV_C):
                    dve.wait_ge(kv_turned.sem, kv_turned.at(c + 1))
                    k, f = c // KVH, slice(c % KVH * P, (c % KVH + 1) * P)
                    dve.tensor_copy(KV[:, 0:2, k, f],
                                    ps[:, c % 4, 0:2 * P].rearrange("p (t n) -> p t n", t=2)).then_inc(
                        kv_moved.sem, kv_moved.inc())
                    dve.tensor_copy(KV[0:NS, 2, k, f], ps[0:NS, c % 4, 2 * P:3 * P]).then_inc(
                        kv_moved.sem, kv_moved.inc())
                dve.wait_ge(bias_moved.sem, bias_moved.at(6))

                def front(u):
                    qt, h = units[u]
                    r, n = u % 2, nk_of(qt)
                    dve.wait_ge(sc_done.sem, sc_done.at(u + 1))
                    if u >= 2:
                        dve.wait_ge(pt_done.sem, pt_done.at(u - 1))
                    bias = BT.rearrange("p h t k -> p h (t k)")[:, h:h + 1, 2 * P - n:2 * P].broadcast_to([P, 2, n])
                    dve.tensor_tensor(
                        Sb[:, r, :, 0:n], ps[:, 2 * r:2 * r + 2, 0:n], bias, ALU.add).then_inc(
                        sc_ready.sem, sc_ready.inc())
                    dve.wait_ge(sc_ready.sem, sc_ready.at(u + 1))
                    dve.tensor_reduce(st[:, r, 0, :], Sb[:, r, :, 0:n], AX.X, ALU.max, negate=True).then_inc(
                        mx_ready.sem, mx_ready.inc())

                def combine(u):
                    qt, h = units[u]
                    r, n = u % 2, nk_of(qt)
                    dve.wait_ge(p_ready.sem, p_ready.at(2 * u + 2))
                    dve.reciprocal(st[:, r, 2, :], st[:, r, 1, :]).then_inc(diag_ready.sem, diag_ready.inc())
                    dve.wait_ge(diag_ready.sem, diag_ready.at(2 * u + 1))
                    dve.tensor_tensor(st[:, r, 1, 1:2], st[:, r, 2, 1:2], lamcol[:, :], ALU.mult).then_inc(
                        diag_ready.sem, diag_ready.inc())
                    dve.tensor_scalar(Sb[:, r, 0, 0:n], Sb[:, r, 0, 0:n], st[:, r, 2, 0:1], None, ALU.mult).then_inc(
                        scaled.sem, scaled.inc())
                    dve.wait_ge(diag_ready.sem, diag_ready.at(2 * u + 2))
                    dve.wait_ge(scaled.sem, scaled.at(2 * u + 1))
                    dve.scalar_tensor_tensor(
                        out=Sb[:, r, 0, 0:n], in0=Sb[:, r, 1, 0:n], scalar=st[:, r, 1, 1:2],
                        in1=Sb[:, r, 0, 0:n], op0=ALU.mult, op1=ALU.add).then_inc(scaled.sem, scaled.inc())

                def out(u):
                    qt, h = units[u]
                    dve.wait_ge(pv_done.sem, pv_done.at(u + 1))
                    dve.tensor_copy(OT[:, h, qt * P:(qt + 1) * P], ps[:, 6 + u % 2, 0:P]).then_inc(
                        o_moved.sem, o_moved.inc())
                front(0)
                for u in range(len(units)):
                    if u + 1 < len(units):
                        front(u + 1)
                    combine(u)
                    if u >= 2:
                        out(u - 2)
                out(len(units) - 2)
                out(len(units) - 1)

        with phase() as (block, sb):
            Kp, Vp = sb("Kp", [P, 2, NPAGES, KVH * P]), sb("Vp", [P, 2, NPAGES, KVH * P])
            KT = sb("KT", [P, KVH, PAST])
            Qall, Qst = sb("Qall", [P, NB, KVH, 32]), sb("Qst", [P, 2, KVH, 32])
            oh = sb("oh", [33, T, PAST + T])
            rb, LT = sb("rb", [33, NH]), sb("LT", [33, T, KVH, 32])
            bias, BN, base = sb("bias", [P, PAST]), sb("BN", [P, NB, NS]), sb("base", [P, T])
            Sb, st, CR = sb("Sb", [P, 2, PAST + NS]), sb("st", [P, 2, 3]), sb("CR", [P, 2, NH * T])
            mapcol = sb("mapcol", [P, 1])
            PT = sb("PT", [P, 2, (NPAGES + 1) * NH * T + 32])
            OS = sb("OS", [P, 2, P])
            ptab = sb("ptab", [1, NB * NPAGES], I32)
            prep, prep2, prep3 = S("buffers_filled"), S("bias_tables"), S("tables_laid")
            comb = cst[:, C_COMB:C_COMB + NH * T]
            W = NH * T
            NEWC = (NPAGES + 1) * W

            @block.sync
            def _(sp):
                sp.dma_start(ptab[:, :], A["page_table"].rearrange("b n -> (b n)").rearrange(
                    "(a n) -> a n", a=1)).then_inc(table_in.sem, table_in.inc())
                sp.dma_start(oh[:, :, :], A["onehot_diff"]).then_inc(loaded.sem, loaded.inc())
                sp.dma_start(rb[0:32, :], A["rel_bias"]).then_inc(loaded.sem, loaded.inc())
                sp.wait_ge(table_in.sem, table_in.at(1))
                n_pages = A["cache_diff_k"].shape[1]

                def load(dst, cache, r, pages, arrived):
                    for j in range(NPAGES):
                        sp.dma_start(dst[:, r, j, :], kv_pages(cache)[ds(pages[j], 1)].rearrange(
                            "a p n -> p (a n)")).then_inc(arrived.sem, arrived.inc())
                for b in range(NB):
                    r = b % 2
                    pages = [sp.value_load(ptab[0:1, b * NPAGES + j:b * NPAGES + j + 1],
                                           min_val=0, max_val=n_pages - 1) for j in range(NPAGES)]
                    if b >= 2:
                        sp.wait_ge(k_turned.sem, k_turned.at(4 * (b - 1)))
                    load(Kp, A["cache_diff_k"], r, pages, pages_in[r])
                    if b >= 2:
                        sp.wait_ge(pv_done.sem, pv_done.at(b - 1))
                    load(Vp, A["cache_diff_v"], r, pages, values_in[r])

            @block.gpsimd
            def _(pool):
                pool.memset(Qall[:, :, :, :], 0.0).then_inc(prep.sem, prep.inc())
                pool.memset(PT[:, :, :], 0.0).then_inc(prep.sem, prep.inc())
                pool.memset(LT[:, :, :, :], 0.0).then_inc(prep.sem, prep.inc())
                pool.memset(BN[:, :, :], NEG).then_inc(prep.sem, prep.inc())
                pool.wait_ge(prep3.sem, prep3.at(9))
                with repeat(pool, NB // 2) as it:
                    for r in range(2):
                        b = it * 2 + r
                        pool.wait_ge(old_scored.sem, old_scored.at(b - 1))
                        pool.tensor_copy(Qst[:, r:r + 1, :, :], Qall[:, ds(b, 1), :, :]).then_inc(
                            q_staged.sem, q_staged.inc())

            @block.tensor
            def _(pe):
                pe.wait_ge(prep3.sem, prep3.at(17))
                for lo, n, out in ((0, 512, ps[:, 4, :]), (512, 512, ps[:, 5, :]), (PAST, T, ps[:, 6, 0:T])):
                    for t in range(T):
                        mm = pe.matmul(out, LT[:, t, :, :].rearrange("p g n -> p (g n)"), oh[:, t, lo:lo + n],
                                       start=(t == 0), stop=(t == T - 1))
                mm.then_inc(prep2.sem, prep2.inc())

                def turn_keys(b, r, g):
                    pe.wait_ge(k_moved_a.sem, k_moved_a.at(4 * b + (g - 1)))
                    pe.wait_ge(k_moved_v.sem, k_moved_v.at(4 * b + (g - 1)))
                    for j in range(NPAGES):
                        mm = pe.transpose(ps[:, 2 * (g % 2) + j // 4, j % 4 * P:(j % 4 + 1) * P],
                                          Kp[:, r, j, g * P:(g + 1) * P], ident)
                    mm.then_inc(k_turned.sem, k_turned.inc())

                def scores(b, r, g):
                    pe.wait_ge(k_moved_a.sem, k_moved_a.at(4 * b + (g + 1)))
                    pe.wait_ge(k_moved_v.sem, k_moved_v.at(4 * b + (g + 1)))
                    for half in range(2):
                        pe.matmul(ps[32 * g:32 * g + 32, 4 + half, :], Qst[:, r, g, :],
                                  KT[:, g, half * 512:half * 512 + 512], start=True, stop=True,
                                  tile_position=(0, 32 * g))

                def turn_probs(b, r):
                    pe.wait_ge(diag_ready.sem, diag_ready.at(2 * b + 2))
                    for n in range(NPAGES + 1):
                        k = P if n < NPAGES else NS
                        mm = pe.matmul(ps[0:k, 6, W * n:W * n + W], Sb[:, r, P * n:P * n + k], CR[:, r, :],
                                       start=True, stop=True)
                    mm.then_inc(pt_done.sem, pt_done.inc())

                def values(b, r, half):
                    pe.wait_ge(values_in[r].sem, values_in[r].at(NPAGES * (half + 1)))
                    pe.wait_ge(o_moved.sem, o_moved.at(b))
                    pe.wait_ge(pt_moved.sem, pt_moved.at(2 * b + 2))
                    for g in range(KVH):
                        for n in range(NPAGES + 1):
                            v = Vp[:, r, n, g * P:(g + 1) * P] if n < NPAGES else KV[0:NS, 2, 1, g * P:(g + 1) * P]
                            k, o = (P if n < NPAGES else NS), W * n + g * REP * T
                            mm = pe.matmul(ps[32 * g:32 * g + 32, 7, 0:P], PT[0:k, r, o:o + 32], v,
                                           start=(n == 0), stop=(n == NPAGES), tile_position=(0, 32 * g))
                    mm.then_inc(pv_done.sem, pv_done.inc())

                def turn_out(b, r):
                    pe.wait_ge(out_staged.sem, out_staged.at(b + 1))
                    pe.transpose(ps[:, 7, P:2 * P], OS[:, r, :], ident).then_inc(out_turned.sem, out_turned.inc())

                def front(b, r, half, back, before):
                    pe.wait_ge(pages_in[r].sem, pages_in[r].at(NPAGES * (half + 1)))
                    turn_keys(b, r, 0)
                    if before:
                        turn_out(b - 2, r)
                    turn_keys(b, r, 1)
                    pe.wait_ge(q_staged.sem, q_staged.at(b + 1))
                    pe.wait_ge(sc_ready.sem, sc_ready.at(3 * b))
                    scores(b, r, 0)
                    turn_keys(b, r, 2)
                    scores(b, r, 1)
                    if back:
                        turn_probs(b - 1, 1 - r)
                    turn_keys(b, r, 3)
                    scores(b, r, 2)
                    scores(b, r, 3)
                    pe.wait_ge(pt_moved.sem, pt_moved.at(2 * b))
                    for g in range(KVH):
                        mm = pe.matmul(ps[32 * g:32 * g + 32, 6, NEWC:NEWC + NS], Qst[:, r, g, :],
                                       X[:, QD_C + g, SEQ:TOK], start=True, stop=True, tile_position=(0, 32 * g))
                    mm.then_inc(old_scored.sem, old_scored.inc())
                    if back:
                        values(b - 1, 1 - r, half - (1 - r))
                pe.wait_ge(prep2.sem, prep2.at(3))
                front(0, 0, 0, False, False)
                front(1, 1, 0, True, False)
                with repeat(pe, NB // 2 - 1) as it:
                    for r in range(2):
                        front(it * 2 + (r + 2), r, it + 1, True, True)
                turn_out(NB - 2, 0)
                turn_probs(NB - 1, 1)
                values(NB - 1, 1, NB // 2 - 1)
                turn_out(NB - 1, 1)

            @block.scalar
            def _(act):
                def front(b, r, back):
                    if back:
                        act.wait_ge(mx_ready.sem, mx_ready.at(b))
                        act.activation(Sb[:, 1 - r, :], Sb[:, 1 - r, :], ACT.Exp,
                                       bias=st[:, 1 - r, 0:1], accum_out=st[:, 1 - r, 1:2]).then_inc(
                            p_ready.sem, p_ready.inc())
                    for g in range(KVH):
                        act.wait_ge(k_turned.sem, k_turned.at(4 * b + (g + 1)))
                        act.activation(KT[:, g, 0:512], ps[:, 2 * (g % 2), :], ACT.Copy).then_inc(
                            k_moved_a.sem, k_moved_a.inc())
                front(0, 0, False)
                with repeat(act, NB // 2 - 1) as it:
                    for r in (1, 0):
                        front(it * 2 + (2 - r), r, True)
                front(NB - 1, 1, True)
                act.wait_ge(mx_ready.sem, mx_ready.at(NB))
                act.activation(Sb[:, 1, :], Sb[:, 1, :], ACT.Exp,
                               bias=st[:, 1, 0:1], accum_out=st[:, 1, 1:2]).then_inc(p_ready.sem, p_ready.inc())

            @block.vector
            def _(dve):
                dve.memset(rb[32:33, :], NEG).then_inc(prep3.sem, prep3.inc())
                dve.wait_ge(prep.sem, prep.at(4))
                for m in range(2):
                    for g in range(KVH):
                        rows = slice(64 * m, 64 * m + 64)
                        c0 = m * REP * T
                        dve.tensor_copy(
                            Qall[rows, :, g, c0:c0 + REP * T].rearrange("p b (r t) -> p b r t", t=T),
                            X[rows, REP * g:REP * g + REP, SEQ:TOK].rearrange("p r (b t) -> p b r t", t=T)).then_inc(
                            prep3.sem, prep3.inc())
                dve.wait_ge(loaded.sem, loaded.at(2))
                dve.wait_ge(prep3.sem, prep3.at(1))
                for t in range(T):
                    for m in range(2):
                        c0 = m * REP * T
                        dve.tensor_copy(LT[:, t, :, c0 + t:c0 + REP * T:T],
                                        rb.rearrange("p (g r) -> p g r", g=KVH)).then_inc(prep3.sem, prep3.inc())
                dve.scalar_tensor_tensor(
                    out=mapcol[:, :], in0=cst[:, C_COMB + W + 1:C_COMB + W + 2], scalar=lamcol[:, 0:1],
                    in1=cst[:, C_COMB + W:C_COMB + W + 1], op0=ALU.mult, op1=ALU.add).then_inc(prep3.sem, prep3.inc())
                dve.wait_ge(prep2.sem, prep2.at(1))
                dve.tensor_copy(bias.rearrange("p (a n) -> p a n", a=2), ps[:, 4:6, :]).then_inc(prep2.sem, prep2.inc())
                dve.tensor_copy(base[:, :], ps[:, 6, 0:T]).then_inc(prep2.sem, prep2.inc())
                dve.wait_ge(prep2.sem, prep2.at(3))
                for b in range(NB):
                    dve.tensor_copy(BN[:, b, b * T:(b + 1) * T], base[:, :]).then_inc(prep3.sem, prep3.inc())
                dve.wait_ge(prep3.sem, prep3.at(26))

                def keys(b, g):
                    dve.wait_ge(k_turned.sem, k_turned.at(4 * b + (g + 1)))
                    dve.tensor_copy(KT[:, g, 512:PAST], ps[:, 2 * (g % 2) + 1, :]).then_inc(
                        k_moved_v.sem, k_moved_v.inc())

                def scale(b, r):
                    dve.wait_ge(p_ready.sem, p_ready.at(b + 1))
                    dve.reciprocal(st[:, r, 2:3], st[:, r, 1:2]).then_inc(diag_ready.sem, diag_ready.inc())
                    dve.wait_ge(diag_ready.sem, diag_ready.at(2 * b + 1))
                    dve.tensor_scalar(CR[:, r, :], comb, st[:, r, 2:3], mapcol[:, 0:1],
                                      ALU.mult, ALU.mult).then_inc(diag_ready.sem, diag_ready.inc())

                def probs(b, r):
                    dve.wait_ge(pt_done.sem, pt_done.at(b + 1))
                    dve.tensor_copy(PT[:, r, 0:NPAGES * W], ps[:, 6, 0:NPAGES * W]).then_inc(
                        pt_moved.sem, pt_moved.inc())
                    dve.tensor_copy(PT[0:NS, r, NPAGES * W:NEWC], ps[0:NS, 6, NPAGES * W:NEWC]).then_inc(
                        pt_moved.sem, pt_moved.inc())

                def stage_out(b, r):
                    dve.wait_ge(pv_done.sem, pv_done.at(b + 1))
                    dve.tensor_copy(OS[:, r, :], ps[:, 7, 0:P]).then_inc(out_staged.sem, out_staged.inc())

                def out(b):
                    dve.wait_ge(out_turned.sem, out_turned.at(b + 1))
                    dve.tensor_copy(OT[:, :, ds(b * T + SEQ, T)].rearrange("p (g r) t -> p g r t", g=KVH),
                                    ps[:, 7, P:2 * P].rearrange("p (g n) -> p g n", g=KVH)[:, :, 0:REP * T].rearrange(
                                        "p g (r t) -> p g r t", t=T)).then_inc(o_moved.sem, o_moved.inc())

                def front(b, r, back, before):
                    keys(b, 0)
                    if before:
                        out(b - 2)
                    if back:
                        scale(b - 1, 1 - r)
                    keys(b, 1)
                    keys(b, 2)
                    if back:
                        probs(b - 1, 1 - r)
                    keys(b, 3)
                    dve.wait_ge(old_scored.sem, old_scored.at(b + 1))
                    dve.wait_ge(pt_done.sem, pt_done.at(b - 1))
                    for half in range(2):
                        lo = half * 512
                        dve.tensor_tensor(Sb[:, r, lo:lo + 512], ps[:, 4 + half, :],
                                          bias[:, lo:lo + 512], ALU.add).then_inc(sc_ready.sem, sc_ready.inc())
                    dve.tensor_tensor(Sb[:, r:r + 1, PAST:PAST + NS], ps[:, 6:7, NEWC:NEWC + NS],
                                      BN[:, ds(b, 1), :], ALU.add).then_inc(sc_ready.sem, sc_ready.inc())
                    dve.wait_ge(sc_ready.sem, sc_ready.at(3 * b + 3))
                    dve.tensor_reduce(st[:, r, 0:1], Sb[:, r, :], AX.X, ALU.max, negate=True).then_inc(
                        mx_ready.sem, mx_ready.inc())
                    if back:
                        stage_out(b - 1, 1 - r)
                front(0, 0, False, False)
                front(1, 1, True, False)
                with repeat(dve, NB // 2 - 1) as it:
                    for r in range(2):
                        front(it * 2 + (r + 2), r, True, True)
                out(NB - 2)
                scale(NB - 1, 1)
                probs(NB - 1, 1)
                stage_out(NB - 1, 1)
                out(NB - 1)

        with phase() as (block, sb):
            act_norm, pe_norm, dve_norm, _ = norm_heads(block, sb, OT, QD_C, 0, V_DOUT, ones, P, 1.0 - LAM_INIT)
            block.scalar(act_norm)
            block.tensor(pe_norm)
            block.vector(dve_norm)

        linear_phase([(Linear(KD, QD_C, 1, columns(A["diff_w_out"][0], QD_C, 1)),
                       lambda sb, parts: residual(sb, parts, QD_C))], nxt, source=lambda c: OT[:, c, :])
        mem.close()

    if order is None:
        order = [("ssd", 0), ("ffn", 0), ("swa", 1), ("ffn", 1), ("diff", 2), ("ffn", 2), ("ssd", 3), ("ffn", 3)]
    firsts = dict(ffn=ffn_first, ssd=ssd_first, swa=swa_first, diff=diff_first)
    nexts = [firsts[kind](layer) for kind, layer in order] + [None]
    with stack:
        setup(nexts[0])
        for n, (kind, layer) in enumerate(order):
            dict(ffn=ffn, ssd=ssd, swa=swa, diff=diff)[kind](layer, nexts[n + 1])
        finish()


def one_hot(dist, seen):
    d = np.maximum(dist, 0)
    f = np.maximum(d, 1).astype(np.float32)
    large = 16 + (np.log(f / np.float32(16)) / np.float32(math.log(2048 / 16)) * np.float32(16)).astype(np.int32)
    bucket = np.where(seen, np.where(d < 16, d, np.minimum(large, 31)), 32)
    return (np.arange(33).reshape(33, *[1] * dist.ndim) == bucket[None]).astype(np.float32)


def shape_constants():
    c = np.zeros((P, C_END), np.float32)
    i = np.arange(P)
    c[:, C_ID:C_ID + P] = np.eye(P)
    c[:, C_ONE:C_ONE + P] = 1
    c[:, C_BLK:C_BLK + P] = i[:, None] // HD == i[None] // HD
    c[:, C_ANTI:C_ANTI + P] = i[:, None] + i[None] == P - 1
    c[:, C_TRI:C_TRI + P] = i[:, None] <= i[None]
    s = i[:NS]
    same = s[:, None] // T == s[None] // T
    c[:NS, C_TRIS:C_TRIS + NS] = same & (s[:, None] <= s[None])
    c[:NS, C_SAME:C_SAME + NS] = same
    c[:NS, C_BCOL:C_BCOL + NB] = s[:, None] // T == np.arange(NB)[None]
    g, m, q = i // 32, i % 32 // 12, i % 32 % 12
    c[:, C_COMB:C_COMB + 48] = (m[:, None] < 2) & ((g * 12 + q)[:, None] == np.arange(48)[None])
    c[:, C_COMB + 48], c[:, C_COMB + 49] = m == 0, m == 1
    dist = np.arange(512) - (P - 1)
    tabs = [one_hot(dist, (dist >= 0) & (dist <= win) & (dist % dil == 0)) for win, dil in WINDOWS]
    tabs.append(one_hot(dist, dist >= 0))
    t = np.arange(T)[:, None]
    parts = []
    for (win, dil), held, pos in ((WINDOWS[1], 512, np.arange(512)), (WINDOWS[0], 128, np.arange(128)),
                                  (WINDOWS[2], PAST, (np.arange(4)[:, None] + 16 * np.arange(64)[None]).ravel())):
        d = held + t - pos[None]
        parts.append(one_hot(d, (d >= 0) & (d <= win) & (d % dil == 0)))
    d = t - np.arange(T)[None]
    for win, dil in WINDOWS:
        parts.append(one_hot(d, (d >= 0) & (d % dil == 0)))
    dd = PAST + t - np.arange(PAST + T)[None]
    return {"constants": c, "onehot_dist": np.stack(tabs, axis=1), "onehot_swa": np.concatenate(parts, axis=2),
            "onehot_diff": one_hot(dd, dd >= 0)}


_INS = ["x_prompt", "x_sample", "state_ssm_conv", "state_ssm", "cache_swa_kv0", "cache_swa_kv1", "cache_swa_kv2",
        "cache_diff_k", "cache_diff_v", "page_table", "rel_bias", "norm_mix", "norm_ffn", "ffn_w_in", "ffn_w_out",
        "ssm_w_in", "ssm_conv_w", "ssm_conv_b", "ssm_dt_bias", "ssm_a_log", "ssm_d", "ssm_norm", "ssm_w_out",
        "swa_w_qkv", "swa_q_norm", "swa_k_norm", "swa_w_out",
        "diff_w_qkv", "diff_q_norm", "diff_k_norm", "diff_lambda", "diff_out_norm", "diff_w_out"]
_OUTS = {
    "y_prompt": (1, SEQ, D_MODEL), "y_sample": (NB, T, D_MODEL),
    "ssm_conv_prompt": (2, 1, 3, CONV_DIM), "ssm_conv_sample": (2, NB, 3, CONV_DIM),
    "ssm_prompt": (2, 1, HEADS, 64, N_STATE), "ssm_sample": (2, NB, HEADS, 64, N_STATE),
    "swa_kv0_prompt": (1, 1, 128, 2, GH, HD), "swa_kv0_sample": (1, NB, 128, 2, GH, HD),
    "swa_kv1_prompt": (1, 1, 256, 2, GH, HD), "swa_kv1_sample": (1, NB, 512, 2, GH, HD),
    "swa_kv2_prompt": (1, 1, 256, 2, GH, HD), "swa_kv2_sample": (1, NB, PAST + T, 2, GH, HD),
    "diff_k_prompt": (1, 1, SEQ, KVH, 2, HD), "diff_k_sample": (1, NB, T, KVH, 2, HD),
    "diff_v_prompt": (1, 1, SEQ, KVH, 2 * HD), "diff_v_sample": (1, NB, T, KVH, 2 * HD),
}


def kernel(**inputs):
    import concourse.bacc as _bacc
    from concourse.bass_utils import run_bass_kernel_spmd as _run

    nc = _bacc.Bacc("TRN2", target_bir_lowering=False, num_devices=1)
    arrays, A, O = {}, {}, {}
    for name in _INS + list(shape_constants()):
        a = np.ascontiguousarray(inputs[name] if name in inputs else shape_constants()[name])
        arrays[f"in_{name}"] = a
        A[name] = nc.dram_tensor(f"in_{name}", a.shape, mybir.dt.from_np(a.dtype), kind="ExternalInput").ap()
    for name, shape in _OUTS.items():
        O[name] = nc.dram_tensor(f"out_{name}", shape, F32, kind="ExternalOutput").ap()
    build_program(nc, A, O)
    r = _run(nc, [arrays], core_ids=[0])
    return tuple(r.results[0][f"out_{name}"] for name in _OUTS)
```
